# Optimizing a Trainium2 kernel written in Bass

```python
import math
import jax, jax.numpy as jnp
from jax import lax
import numpy as np

D_MODEL = 1024
BATCH = 1
SEQ = 512
DEPTH = 1

MEM_LEN = 256
ATT_W = D_MODEL // 2
ATT_HD = 64
ATT_HEADS = ATT_W // ATT_HD
DILATED = ((128, 1), (512, 4), (2048, 16))
BLK = 128
ML_W = D_MODEL // 2
ML_HEADS = 4
ML_HD = ML_W // ML_HEADS
CHUNK = 128
CONV_K = 4
MIX_W = ATT_W + ML_W
SPLITS = [ATT_W, 2 * ATT_W, 3 * ATT_W, 3 * ATT_W + 2 * ML_W, 3 * ATT_W + 3 * ML_W, 3 * ATT_W + 4 * ML_W]
W_IN = 3 * ATT_W + 4 * ML_W + 2 * ML_HEADS
XA_HEADS = 4
XA_HD = D_MODEL // XA_HEADS
D_FF = ((8 * D_MODEL // 3 + 255) // 256) * 256
REL_BUCKETS = 32
REL_MAX_DIST = 2048
ALPHA = (2 * DEPTH) ** 0.25
BETA = (8 * DEPTH) ** -0.25
LN_EPS = 1e-5
NEG = -1e30

kernel_name = 'hymba_dilated_mlstm_macaron_deepnorm'

def layer_norm(x, g, b):
    xf = x.astype(jnp.float32)
    mu = jnp.mean(xf, -1, keepdims=True)
    var = jnp.mean(jnp.square(xf - mu), -1, keepdims=True)
    y = (xf - mu) * lax.rsqrt(var + LN_EPS)
    return (y * g.astype(jnp.float32) + b.astype(jnp.float32)).astype(x.dtype)

def swiglu(x, w_gate, w_up, w_down):
    return (jax.nn.silu(x @ w_gate) * (x @ w_up)) @ w_down

def t5_bucket(dist):
    exact = REL_BUCKETS // 2
    df = jnp.maximum(dist, 1).astype(jnp.float32)
    large = exact + (jnp.log(df / exact) / math.log(REL_MAX_DIST / exact) * (REL_BUCKETS - exact)).astype(jnp.int32)
    large = jnp.minimum(large, REL_BUCKETS - 1)
    return jnp.where(dist < exact, dist, large)

def band_offsets():
    qi = jnp.arange(BLK)[:, None]
    ki = jnp.arange(2 * BLK)[None, :]
    return qi + BLK - ki, ki

def branch_bias(rel_table, dilation, n_keys):
    off, _ = band_offsets()
    bucket = t5_bucket(dilation * jnp.clip(off, 0, n_keys))
    return jnp.transpose(rel_table.astype(jnp.float32)[bucket], (2, 0, 1))

def banded_attention(q, k, v, bias, n_keys):
    B, H, R, M, E = q.shape
    nb = M // BLK
    blocks = lambda t: t.reshape(B, H, R, nb, BLK, E)
    shift = lambda t: jnp.concatenate([jnp.zeros_like(t[:, :, :, :1]), t[:, :, :, :-1]], axis=3)
    qb, kb, vb = blocks(q), blocks(k), blocks(v)
    kk = jnp.concatenate([shift(kb), kb], axis=4)
    vv = jnp.concatenate([shift(vb), vb], axis=4)
    logits = jnp.einsum('bhrnqe,bhrnke->bhrnqk', qb, kk).astype(jnp.float32) * (ATT_HD ** -0.5)
    logits = logits + bias[:, None, None]
    off, ki = band_offsets()
    band = (off >= 0) & (off <= n_keys)
    valid = band[None] & ((jnp.arange(nb)[:, None, None] > 0) | (ki[None] >= BLK))
    logits = jnp.where(valid, logits, NEG)
    mx = jnp.max(logits, -1, keepdims=True)
    p = jnp.exp(logits - mx)
    s = jnp.sum(p, -1)
    o = jnp.einsum('bhrnqk,bhrnke->bhrnqe', p, vv) / s[..., None]
    lse = mx[..., 0] + jnp.log(s)
    return o.reshape(B, H, R, M, E), lse.reshape(B, H, R, M)

def dilated_branch(q, k, v, rel_table, window, dilation):
    B, H, S, E = q.shape
    span = dilation * BLK
    s_pad = -(-S // span) * span
    m_len = s_pad // dilation
    n_keys = window // dilation

    def fold(t):
        t = jnp.pad(t, ((0, 0), (0, 0), (0, s_pad - S), (0, 0)))
        return t.reshape(B, H, m_len, dilation, E).transpose(0, 1, 3, 2, 4)

    o, lse = banded_attention(fold(q), fold(k), fold(v), branch_bias(rel_table, dilation, n_keys), n_keys)
    o = o.transpose(0, 1, 3, 2, 4).reshape(B, H, s_pad, E)[:, :, :S]
    lse = lse.transpose(0, 1, 3, 2).reshape(B, H, s_pad)[:, :, :S]
    return o, lse

def dilated_attention(q, k, v, rel_table):
    outs, lses = [], []
    for window, dilation in DILATED:
        o, l = dilated_branch(q, k, v, rel_table, window, dilation)
        outs.append(o)
        lses.append(l)
    wts = jax.nn.softmax(jnp.stack(lses, 0), axis=0)
    return jnp.sum(wts[..., None] * jnp.stack(outs, 0), 0)

def causal_conv(x, w, b):
    S = x.shape[1]
    xp = jnp.pad(x, ((0, 0), (CONV_K - 1, 0), (0, 0)))
    y = b
    for j in range(CONV_K):
        y = y + xp[:, j:j + S] * w[j]
    return y

def mlstm(q, k, v, ig, fg):
    B, H, S, E = q.shape
    nc = S // CHUNK
    ch = lambda t: t.reshape(B, H, nc, CHUNK, E)
    q, k, v = ch(q), ch(k) * (E ** -0.5), ch(v)
    ig = ig.astype(jnp.float32).reshape(B, H, nc, CHUNK)
    logf = jax.nn.log_sigmoid(fg.astype(jnp.float32)).reshape(B, H, nc, CHUNK)
    b = jnp.cumsum(logf, -1)
    g = b[..., -1]
    a = g[..., None] - b + ig
    m_loc = jnp.max(a, -1)
    wa = jnp.exp(a - m_loc[..., None])
    c_loc = jnp.einsum('bhcl,bhcld,bhcle->bhcde', wa, v, k)
    n_loc = jnp.einsum('bhcl,bhcle->bhce', wa, k)

    def step(carry, inp):
        c, n, m = carry
        g_c, cl, nl, ml = inp
        m_new = jnp.maximum(g_c + m, ml)
        sp = jnp.exp(g_c + m - m_new)
        sl = jnp.exp(ml - m_new)
        c_new = sp[..., None, None] * c + sl[..., None, None] * cl
        n_new = sp[..., None] * n + sl[..., None] * nl
        return (c_new, n_new, m_new), (c, n, m)

    init = (jnp.zeros((B, H, E, E), jnp.float32), jnp.zeros((B, H, E), jnp.float32), jnp.zeros((B, H), jnp.float32))
    mv = lambda t: jnp.moveaxis(t, 2, 0)
    _, (c_prev, n_prev, m_prev) = lax.scan(step, init, (mv(g), mv(c_loc), mv(n_loc), mv(m_loc)))
    c_prev = jnp.moveaxis(c_prev, 0, 2)
    n_prev = jnp.moveaxis(n_prev, 0, 2)
    m_prev = jnp.moveaxis(m_prev, 0, 2)

    causal = jnp.tril(jnp.ones((CHUNK, CHUNK), bool))
    d_log = jnp.where(causal, b[..., :, None] - b[..., None, :] + ig[..., None, :], -jnp.inf)
    e_log = b + m_prev[..., None]
    m_t = jnp.maximum(e_log, jnp.max(d_log, -1))
    d_w = jnp.exp(d_log - m_t[..., None])
    e_w = jnp.exp(e_log - m_t)
    s_qk = jnp.einsum('bhcte,bhcse->bhcts', q, k) * d_w
    num = e_w[..., None] * jnp.einsum('bhcde,bhcte->bhctd', c_prev, q) + jnp.einsum('bhcts,bhcsd->bhctd', s_qk, v)
    den = e_w * jnp.einsum('bhce,bhcte->bhct', n_prev, q) + jnp.sum(s_qk, -1)
    h = num / jnp.maximum(jnp.abs(den), jnp.exp(-m_t))[..., None]
    return h.reshape(B, H, S, E)

def head_norm(h, g, n_heads):
    B, S, W = h.shape
    hf = h.astype(jnp.float32).reshape(B, S, n_heads, W // n_heads)
    mu = jnp.mean(hf, -1, keepdims=True)
    var = jnp.mean(jnp.square(hf - mu), -1, keepdims=True)
    y = ((hf - mu) * lax.rsqrt(var + LN_EPS)).reshape(B, S, W)
    return y * g.astype(jnp.float32)

def hybrid_mixer(x, w_in, conv_w, conv_b, ig_b, fg_b, ml_g, w_out, rel_table):
    B, S, _ = x.shape
    proj = x @ w_in
    qa, ka, va, qk_m, vm, om, gates = jnp.split(proj, SPLITS, axis=-1)
    heads = lambda t, h: t.reshape(B, S, h, -1).transpose(0, 2, 1, 3)
    att = dilated_attention(heads(qa, ATT_HEADS), heads(ka, ATT_HEADS), heads(va, ATT_HEADS), rel_table)
    att = att.transpose(0, 2, 1, 3).reshape(B, S, ATT_W).astype(x.dtype)
    qk_m = jax.nn.silu(causal_conv(qk_m, conv_w, conv_b))
    qm, km = jnp.split(qk_m, 2, axis=-1)
    ig = (gates[..., :ML_HEADS] + ig_b).transpose(0, 2, 1)
    fg = (gates[..., ML_HEADS:] + fg_b).transpose(0, 2, 1)
    h = mlstm(heads(qm, ML_HEADS), heads(km, ML_HEADS), heads(vm, ML_HEADS), ig, fg)
    h = h.transpose(0, 2, 1, 3).reshape(B, S, ML_W)
    h = jax.nn.sigmoid(om.astype(jnp.float32)) * h
    h = head_norm(h, ml_g, ML_HEADS).astype(x.dtype)
    return jnp.concatenate([att, h], axis=-1) @ w_out

def memory_attention(x, mem, wq, wkv, wo):
    B, S, _ = x.shape
    L = mem.shape[1]
    q = (x @ wq).reshape(B, S, XA_HEADS, XA_HD)
    kv = (mem @ wkv).reshape(B, L, 2, XA_HEADS, XA_HD)
    k, v = kv[:, :, 0], kv[:, :, 1]
    logits = jnp.einsum('bshe,bmhe->bhsm', q, k).astype(jnp.float32) * (XA_HD ** -0.5)
    p = jax.nn.softmax(logits, axis=-1)
    o = jnp.einsum('bhsm,bmhe->bshe', p, v).reshape(B, S, D_MODEL).astype(x.dtype)
    return o @ wo

def setup_inputs(seed: int = 0) -> dict:
    key = jax.random.key(seed)
    ks = jax.random.split(key, 20)
    f32 = jnp.float32
    nrm = lambda k, shape, scale: jax.random.normal(k, shape, f32) * scale
    return {
        'x': nrm(ks[0], (BATCH, SEQ, D_MODEL), 1.0),
        'mem': nrm(ks[1], (BATCH, MEM_LEN, D_MODEL), 1.0),
        'rel_bias': nrm(ks[2], (REL_BUCKETS, ATT_HEADS), 0.1),
        'ln_g': 1.0 + nrm(ks[3], (DEPTH, 4, D_MODEL), 0.02),
        'ln_b': nrm(ks[4], (DEPTH, 4, D_MODEL), 0.02),
        'ffn_w_gate': nrm(ks[5], (DEPTH, 2, D_MODEL, D_FF), D_MODEL ** -0.5),
        'ffn_w_up': nrm(ks[6], (DEPTH, 2, D_MODEL, D_FF), D_MODEL ** -0.5),
        'ffn_w_down': nrm(ks[7], (DEPTH, 2, D_FF, D_MODEL), BETA * D_FF ** -0.5),
        'w_in': nrm(ks[8], (DEPTH, D_MODEL, W_IN), D_MODEL ** -0.5),
        'conv_w': nrm(ks[9], (DEPTH, CONV_K, 2 * ML_W), CONV_K ** -0.5),
        'conv_b': nrm(ks[10], (DEPTH, 2 * ML_W), 0.02),
        'ig_bias': nrm(ks[11], (DEPTH, ML_HEADS), 0.1),
        'fg_bias': jnp.linspace(3.0, 6.0, ML_HEADS, dtype=f32)[None] + nrm(ks[12], (DEPTH, ML_HEADS), 0.1),
        'ml_norm_g': 1.0 + nrm(ks[13], (DEPTH, ML_W), 0.02),
        'w_out': nrm(ks[14], (DEPTH, MIX_W, D_MODEL), BETA * MIX_W ** -0.5),
        'xq_w': nrm(ks[15], (DEPTH, D_MODEL, D_MODEL), D_MODEL ** -0.5),
        'xkv_w': nrm(ks[16], (DEPTH, D_MODEL, 2 * D_MODEL), D_MODEL ** -0.5),
        'xo_w': nrm(ks[17], (DEPTH, D_MODEL, D_MODEL), BETA * D_MODEL ** -0.5),
    }

def reference(x, mem, rel_bias, ln_g, ln_b, ffn_w_gate, ffn_w_up, ffn_w_down, w_in, conv_w, conv_b,
              ig_bias, fg_bias, ml_norm_g, w_out, xq_w, xkv_w, xo_w):
    for l in range(DEPTH):
        x = layer_norm(ALPHA * x + 0.5 * swiglu(x, ffn_w_gate[l, 0], ffn_w_up[l, 0], ffn_w_down[l, 0]), ln_g[l, 0], ln_b[l, 0])
        x = layer_norm(ALPHA * x + hybrid_mixer(x, w_in[l], conv_w[l], conv_b[l], ig_bias[l], fg_bias[l],
                                                ml_norm_g[l], w_out[l], rel_bias), ln_g[l, 1], ln_b[l, 1])
        x = layer_norm(ALPHA * x + memory_attention(x, mem, xq_w[l], xkv_w[l], xo_w[l]), ln_g[l, 2], ln_b[l, 2])
        x = layer_norm(ALPHA * x + 0.5 * swiglu(x, ffn_w_gate[l, 1], ffn_w_up[l, 1], ffn_w_down[l, 1]), ln_g[l, 3], ln_b[l, 3])
    return x


_drawn_inputs = setup_inputs


def setup_inputs(seed=0):
    import zlib

    import numpy as np

    out = dict(_drawn_inputs(seed))
    spreads = {}
    factors = {'rel_bias': 8.0, 'conv_b': 8.0, 'ig_bias': 8.0, 'ml_norm_g': 8.0}
    for name, (base, spread) in spreads.items():
        noise = np.random.default_rng([zlib.crc32(name.encode()), seed]).standard_normal(out[name].shape)
        drawn = base * np.exp(spread * noise) if base else spread * noise
        out[name] = __import__('jax').numpy.asarray(drawn.astype(out[name].dtype))
    for name, factor in factors.items():
        out[name] = (out[name] * factor).astype(out[name].dtype)
    return out
```

```python
import math
from contextlib import ExitStack

import concourse.bass as bass
from concourse import mybir

F32 = mybir.dt.float32
F32R = mybir.dt.float32r
ALU = mybir.AluOpType
ACT = mybir.ActivationFunctionType
AXX = mybir.AxisListType.X

P = 128
LN_EPS = 1e-5
ALPHA = 2 ** 0.25

RAW = 3
SPL = 6
AHEAD = 4
TAIL = 4
PTS = 5


def lin(const, per, i):
    return const if i is None else const + i * per


class Steps:

    def __init__(self, eng, sem):
        self.eng, self.sem, self.base, self.k = eng, sem, 0, 0

    def inc(self, ins):
        self.k += 1
        ins.then_inc(self.sem, 1)

    def link(self, ins):
        self.inc(ins)
        self.eng.wait_ge(self.sem, self.base + self.k)

    def enter(self, i, per):
        self.outer = self.base + self.k
        self.base, self.k = self.outer + i * per, 0

    def leave(self, rounds, per):
        assert self.k == per, (self.k, per)
        self.base, self.k = self.outer + rounds * per, 0


def macaron_layer(nc, x, mem, rel_bias, ln_g, ln_b, w_gate, w_up, w_down, w_in, conv_w, conv_b,
                  ig_bias, fg_bias, ml_g, w_out, xq_w, xkv_w, xo_w, onehot, lnm, bias_rows, out):
    S, D = x.shape[1], x.shape[2]
    FF = w_gate.shape[3]
    KT = D // P
    NB = S // P
    MB = mem.shape[1] // P
    FT = FF // P
    AH = rel_bias.shape[1]
    AW = D // 2
    HD = AW // AH
    PAIRS = AH // 2
    MH = ig_bias.shape[1]
    MW = D // 2
    XH = 4
    XSCALE = (D // XH) ** -0.5
    CK = conv_w.shape[1]
    DIST = onehot.shape[1]
    NA = AH * NB
    NX = XH * NB
    assert (S, D, MB, MW // MH, KT, HD, CK) == (512, 1024, 2, P, 8, 64, 4)
    assert FT % 3 == 1 and (FT - TAIL) % SPL == 0 and SPL == 2 * RAW

    U_VA = 3 * FT
    U_QK = U_VA + 4
    U_C0 = U_QK + 2 * PAIRS
    U_VM = U_C0 + 2
    U_C1 = U_VM + 4
    U_OM = U_C1 + 2
    U_C2 = U_OM + 4
    U_WO = U_C2 + 4
    U_XV = U_WO + KT
    U_XK = U_XV + KT
    U_XQ = U_XK + KT
    U_XO = U_XQ + KT
    U_F2 = U_XO + KT
    U_END = U_F2 + 3 * FT
    U_FFN = [0, U_F2]
    DOWN = [(2 * FT, FT, 0), (U_WO, KT, FT), (U_XO, KT, FT + KT), (U_F2 + 2 * FT, FT, FT + 2 * KT)]
    U_CONV = [U_C0, U_C0 + 1, U_C1, U_C1 + 1, U_C2, U_C2 + 1, U_C2 + 2, U_C2 + 3]
    G_QK = NB
    G_C0 = G_QK + 2 * PAIRS
    G_VM = G_C0 + 2
    G_C1 = G_VM + NB
    G_OM = G_C1 + 2
    G_C2 = G_OM + NB
    G_CONV = [G_C0, G_C0 + 1, G_C1, G_C1 + 1, G_C2, G_C2 + 1, G_C2 + 2, G_C2 + 3]

    ctx = ExitStack()
    with ctx:
        KB = 1024
        start = -(-nc.sbuf_base // 64) * 64
        size = (nc.sbuf_usable_end - start) // 64 * 64 - 64
        ctx.enter_context(nc.sbuf_tensor("slab", [P, (size + start - nc.sbuf_base) // 4], F32))
        cursor = [start]

        def at(name, shape, offset, dt=F32):
            return nc.alloc_sbuf_tensor_at(name, shape, dt, offset=offset)

        def sb(name, shape, dt=F32):
            n = 4
            for s in shape[1:]:
                n *= s
            t = at(name, shape, cursor[0], dt)
            cursor[0] += -(-n // 32) * 32
            assert cursor[0] <= start + size, "SBUF is full"
            return t

        xn = sb("xn", [P, NB, D])
        whi = [sb(f"whi{s}", [P, D], F32R) for s in range(SPL)]
        wlo = [sb(f"wlo{s}", [P, D], F32R) for s in range(SPL)]
        raw = [sb(f"raw{s}", [P, D]) for s in range(RAW)]
        ident = sb("ident", [P, P])
        sel = sb("sel", [MH, MH, P])
        mlg = sb("mlg", [P, MW])
        gates = sb("gates", [P, NB, 2 * MH])
        wg_raw = sb("wg_raw", [P, KT, 2 * MH])
        wg_hi = sb("wg_hi", [P, KT, 2 * MH], F32R)
        wg_lo = sb("wg_lo", [P, KT, 2 * MH], F32R)
        gbias = sb("gbias", [MH, 2])
        relb = sb("relb", [rel_bias.shape[0], AH])
        ccol = sb("ccol", [P, CK * KT + KT])
        nmax = sb("nmax", [P, NA])
        rsum = sb("rsum", [P, NA])
        rinv = sb("rinv", [P, NA])
        acol = sb("acol", [P, NB, MH])
        emin = sb("emin", [P, NB, MH])
        den = sb("den", [P, NB])
        hst = sb("hst", [P, NB, 6])
        hmv = sb("hmv", [P, NB, 2])
        hrs = sb("hrs", [P, NB])
        stats = sb("stats", [P, 2, 6])
        mv = sb("mv", [P, NB, 2])
        rstd = sb("rstd", [P, NB])
        eps_col = sb("eps_col", [P, 1])

        gb_at = cursor[0]
        gb = at("gb", [P, 2, D], gb_at)
        craw = [at(f"craw{s}", [P, S + CK - 1], gb_at + s * 2080) for s in range(2)]
        cy = [at(f"cy{s}", [P, S], gb_at + 4160 + s * 2048) for s in range(2)]
        cursor[0] += 4160 + 4096

        hs_at = cursor[0]
        hhi = [at(f"hhi{s}", [P, S], hs_at + s * 4 * KB, F32R) for s in range(SPL)]
        hlo = [at(f"hlo{s}", [P, S], hs_at + s * 4 * KB + 2 * KB, F32R) for s in range(SPL)]
        oh_sb = at("oh_sb", [onehot.shape[0], DIST], hs_at)
        lnm_sb = at("lnm_sb", [AH, DIST], hs_at + 4 * DIST)
        tb_sb = at("tb_sb", [AH, DIST], hs_at + 8 * DIST)
        crow = at("crow", [CK * KT + KT, P], hs_at + 12 * DIST)
        va = at("va", [P, NB, AW], hs_at)
        wb = [at(f"wb{s}", [P, S], hs_at + (8 + 2 * s) * KB) for s in range(2)]
        r_ig = at("r_ig", [MH, S], hs_at + 12 * KB)
        r_f = at("r_f", [MH, S], hs_at + 14 * KB)
        r_a = at("r_a", [MH, S], hs_at + 16 * KB)
        r_e = at("r_e", [MH, S], hs_at + 18 * KB)
        r_one = at("r_one", [MH, S], hs_at + 20 * KB)
        r_sum = at("r_sum", [MH, S], hs_at + 22 * KB)
        lg = [at(f"lg{s}", [P, S], hs_at + (18 + 2 * s) * KB) for s in range(3)]
        cursor[0] += 24 * KB

        ar = cursor[0]
        XTF = [0, ar + 121 * KB // 2]
        xth = [at("xth0", [P, KT, S], ar, F32R), at("xth1", [P, KT, S], ar + 32 * KB, F32R),
               at("xth2", [P, KT, S], ar + 32 * KB, F32R), at("xth3", [P, KT, S], XTF[1], F32R)]
        xtl = [at("xtl0", [P, KT, S], ar + 16 * KB, F32R), at("xtl1", [P, KT, S], ar + 48 * KB, F32R),
               at("xtl2", [P, KT, S], ar + 48 * KB, F32R), at("xtl3", [P, KT, S], XTF[1] + 16 * KB, F32R)]
        hb = [at("h0", [P, FT * S], ar + 32 * KB), at("h1", [P, FT * S], ar)]
        eg = [[at(f"eg0_{s}", [P, S], ar + (76 + 2 * s) * KB) for s in range(3)],
              [at(f"eg1_{s}", [P, S], ar + (44 + 2 * s) * KB) for s in range(3)]]
        mt = at("mt", [P, KT * S], ar)
        qk = [at(f"qk{s}", [P, S], ar + (16 + 2 * s) * KB) for s in range(4)]
        om = at("om", [P, NB, MW], ar + 24 * KB)
        pt = [at(f"pt{s}", [P, S], ar + (64 + 2 * s) * KB) for s in range(PTS)]
        ob = [at(f"ob{s}", [P, NB, P], ar + (74 + 2 * s) * KB) for s in range(2)]
        ew = [at(f"ew{s}", [P, S], ar + (78 + 2 * s) * KB) for s in range(2)]
        vx = at("vx", [P, NB, MH, P + 1], ar + 82 * KB)
        grow = at("grow", [MH, S], ar + 82 * KB + NB * MH * (P + 1) * 4)
        memn = at("memn", [P, MB, D], ar + 32 * KB)
        mth = at("mth", [P, KT, MB * P], ar + 16 * KB, F32R)
        mtl = at("mtl", [P, KT, MB * P], ar + 24 * KB, F32R)
        xpt = [at(f"xpt{s}", [P, MB, S], ar + (16 + 4 * s) * KB) for s in range(2)]
        xp = [at(f"xp{s}", [P, MB * P], ar + (24 + s) * KB) for s in range(3)]
        km = at("km", [P, KT, MB * P], ar + 64 * KB)
        vmem = at("vmem", [P, MB, D], ar + 72 * KB)
        qx = [at(f"qx{s}", [P, S], ar + (80 + 2 * s) * KB) for s in range(4)]
        cursor[0] += 185 * KB // 2
        assert cursor[0] <= start + size, (cursor[0], start + size)

        ps = [ctx.enter_context(nc.psum_tensor(f"ps{b}", [P, 512], F32)) for b in range(8)]

        def sem(name):
            return ctx.enter_context(nc.semaphore(name))

        x_in = [sem(f"x_in{b}") for b in range(NB)]
        raw_in = [sem(f"raw_in{s}") for s in range(RAW)]
        wb_in = [sem(f"wb_in{s}") for s in range(2)]
        small_in = sem("small_in")
        mem_in = sem("mem_in")
        gb_in = sem("gb_in")
        scr_out = sem("scr_out")
        row_out = sem("row_out")
        pool_ok = sem("pool_ok")
        pool_step = sem("pool_step")
        hi_done = sem("hi_done")
        lo_done = sem("lo_done")
        unit_used = sem("unit_used")
        hhi_done = sem("hhi_done")
        hlo_done = sem("hlo_done")
        wg_hi_done = sem("wg_hi_done")
        wg_done = sem("wg_done")
        eg_ready = sem("eg_ready")
        h_done = sem("h_done")
        grp_done = sem("grp_done")
        acc_done = sem("acc_done")
        var_done = sem("var_done")
        rstd_done = sem("rstd_done")
        ln_done = sem("ln_done")
        xtr_done = sem("xtr_done")
        xhi_done = sem("xhi_done")
        xlo_done = sem("xlo_done")
        brow_ready = sem("brow_ready")
        brow_done = sem("brow_done")
        pj_ev = sem("pj_ev")
        gate_mm = sem("gate_mm")
        gate_ev = sem("gate_ev")
        grow_ready = sem("grow_ready")
        fabs_done = sem("fabs_done")
        flog_done = sem("flog_done")
        rows_done = sem("rows_done")
        gcol_ready = sem("gcol_ready")
        acol_done = sem("acol_done")
        emin_done = sem("emin_done")
        lg_ready = sem("lg_ready")
        lg_done = sem("lg_done")
        nmax_done = sem("nmax_done")
        p_done = sem("p_done")
        tr_done = sem("tr_done")
        pt_done = sem("pt_done")
        pv_done = sem("pv_done")
        o_done = sem("o_done")
        ot_done = sem("ot_done")
        mt_ev = sem("mt_ev")
        conv_y = sem("conv_y")
        conv_e = sem("conv_e")
        conv_out = sem("conv_out")
        om_done = sem("om_done")
        gb_ready = sem("gb_ready")
        e_done = sem("e_done")
        em_done = sem("em_done")
        kq_done = sem("kq_done")
        st_done = sem("st_done")
        mpv_done = sem("mpv_done")
        fin1_done = sem("fin1_done")
        hvar_done = sem("hvar_done")
        hr_done = sem("hr_done")
        hn_done = sem("hn_done")
        mtr_done = sem("mtr_done")
        mhi_done = sem("mhi_done")
        mlo_done = sem("mlo_done")
        xv_ev = sem("xv_ev")
        xk_ev = sem("xk_ev")
        xq_ev = sem("xq_ev")
        xl_ready = sem("xl_ready")
        xm_done = sem("xm_done")
        xe_done = sem("xe_done")
        xp_done = sem("xp_done")
        xt_done = sem("xt_done")
        xt_ev = sem("xt_ev")
        xo_ready = sem("xo_ready")
        a_step = sem("a_step")
        v_step = sem("v_step")

        block = ctx.enter_context(nc.Block())

        @block.sync
        def _(sp):
            def cols(w, c0, i=None, per=0):
                v = w.rearrange("(k p) c -> p k c", p=P)
                return v[:, :, c0:c0 + P] if i is None else v[:, :, bass.ds(c0 + i * per, P)]

            def load(c, src, i=None, rearr=True):
                if i is not None or c >= RAW:
                    sp.wait_ge(lo_done, lin(c - RAW + 1, SPL, i))
                dst = raw[c % RAW][:, :]
                if len(src.shape) == 3:
                    dst = dst.rearrange("p (k c) -> p k c", k=src.shape[1])
                sp.dma_start(dst, src).then_inc(raw_in[c % RAW], 16)

            def ffn(n):
                u0 = U_FFN[n]

                def up_tile(j, i=None):
                    load(u0 + 2 * j, cols(w_gate[0, n], j * P, i, 3 * P), i)
                    load(u0 + 2 * j + 1, cols(w_up[0, n], j * P, i, 3 * P), i)

                rounds = FT // 3
                if u0 == 0:
                    for j in range(3):
                        up_tile(j)
                with sp.Fori(0 if u0 else 1, rounds) as i:
                    for j in range(3):
                        up_tile(j, i)
                up_tile(FT - 1)
                d0 = u0 + 2 * FT
                with sp.Fori(0, (FT - TAIL) // SPL) as i:
                    for j in range(SPL):
                        load(d0 + j, w_down[0, n, bass.ds(j * P + i * (SPL * P), P), :], i)
                for k in range(FT - TAIL, FT):
                    load(d0 + k, w_down[0, n, k * P:(k + 1) * P, :])

            for b in range(NB):
                sp.dma_start(xn[:, b, :], x[0, b * P:(b + 1) * P, :]).then_inc(x_in[b], 16)
            ffn(0)

            def rows4(u, c0):
                v = w_in[0, :, c0:c0 + 512].rearrange("(k p) c -> p k c", p=P)
                for t in range(4):
                    load(u + t, v[:, 2 * t:2 * t + 2, :])

            def conv_pair(h):
                load(U_CONV[2 * h], cols(w_in[0], 3 * AW + h * P))
                load(U_CONV[2 * h + 1], cols(w_in[0], 3 * AW + MW + h * P))

            rows4(U_VA, 2 * AW)
            for p in range(PAIRS):
                load(U_QK + 2 * p, cols(w_in[0], p * P))
                load(U_QK + 2 * p + 1, cols(w_in[0], AW + p * P))
            conv_pair(0)
            rows4(U_VM, 3 * AW + 2 * MW)
            conv_pair(1)
            rows4(U_OM, 3 * AW + 3 * MW)
            conv_pair(2)
            conv_pair(3)
            for k in range(KT):
                load(U_WO + k, w_out[0, k * P:(k + 1) * P, :])
            for k in range(KT):
                load(U_XV + k, xkv_w[0, k * P:(k + 1) * P, D:2 * D])
            for t in range(KT):
                load(U_XK + t, cols(xkv_w[0], t * P))
            for t in range(KT):
                load(U_XQ + t, cols(xq_w[0], t * P))
            for k in range(KT):
                load(U_XO + k, xo_w[0, k * P:(k + 1) * P, :])
            ffn(1)
            for b in range(NB):
                sp.wait_ge(ln_done, 3 * NB + b + 1)
                sp.dma_start(out[0, b * P:(b + 1) * P, :], xn[:, b, :]).then_inc(row_out, 16)
            sp.wait_ge(row_out, 16 * NB)

        @block.gpsimd
        def _(pool):
            pool.dma_start(crow[0:CK * KT, :], conv_w[0].rearrange("j (c p) -> (j c) p", p=P)).then_inc(small_in, 16)
            pool.dma_start(crow[CK * KT:, :], conv_b[0].rearrange("(c p) -> c p", p=P)).then_inc(small_in, 16)
            pool.dma_start(oh_sb[:, :], onehot).then_inc(small_in, 16)
            pool.dma_start(relb[:, :], rel_bias).then_inc(small_in, 16)
            pool.dma_start(lnm_sb[:, :], lnm).then_inc(small_in, 16)
            pool.dma_start(gbias[:, 0:1], ig_bias.rearrange("a h -> h a")).then_inc(small_in, 16)
            pool.dma_start(gbias[:, 1:2], fg_bias.rearrange("a h -> h a")).then_inc(small_in, 16)
            pool.dma_start(mlg[:, :], ml_g[0].partition_broadcast(P)).then_inc(small_in, 16)
            pool.dma_start(wg_raw[:, :, :], w_in[0, :, 3 * AW + 4 * MW:].rearrange("(k p) c -> p k c", p=P)).then_inc(small_in, 16)
            nc.gpsimd.memset(ident[:, :], 0.0).then_inc(pool_step, 1)
            nc.gpsimd.memset(sel[:, :, :], 0.0).then_inc(pool_step, 1)
            pool.wait_ge(pool_step, 2)
            nc.gpsimd.affine_select(out=ident[:, :], in_=ident[:, :], compare_op=ALU.not_equal, fill=1.0,
                                    base=0, pattern=[[-1, P]], channel_multiplier=1).then_inc(pool_ok, 1)
            nc.gpsimd.affine_select(out=sel[:, :, :], in_=sel[:, :, :], compare_op=ALU.not_equal, fill=1.0,
                                    base=0, pattern=[[-1, MH], [0, P]], channel_multiplier=1).then_inc(pool_ok, 1)
            nc.gpsimd.memset(vx[:, :, :, :], 1.0).then_inc(pool_ok, 1)

            def load_gb(n):
                pool.dma_start(gb[:, 0, :], ln_g[0, n].partition_broadcast(P)).then_inc(gb_in, 16)
                pool.dma_start(gb[:, 1, :], ln_b[0, n].partition_broadcast(P)).then_inc(gb_in, 16)

            load_gb(0)
            pool.wait_ge(brow_done, 1)
            pool.dma_start(bias_rows, tb_sb[:, :].unsqueeze(1).to_broadcast([AH, P, DIST])).then_inc(scr_out, 16)
            pool.wait_ge(scr_out, 16)
            pool.wait_ge(unit_used, U_VA)
            for h in range(AH):
                if h >= 2:
                    pool.wait_ge(lg_done, NB * (h - 1))
                src = bass.AP(bias_rows.tensor, h * P * DIST + P - 1, [[DIST - 1, P], [1, S]])
                pool.dma_start(wb[h % 2][:, :], src).then_inc(wb_in[h % 2], 16)
            for h in range(MH):
                for j in range(NB):
                    pool.wait_ge(e_done, NB * h + j + 1)
                    blk = ew[j % 2][:, 0:P]
                    nc.gpsimd.affine_select(out=blk, in_=blk, compare_op=ALU.is_ge, fill=0.0, base=0,
                                            pattern=[[1, P]], channel_multiplier=-1).then_inc(em_done, 1)
                if h == 1:
                    pool.wait_ge(conv_out, 2 * MH)
                    load_gb(1)
                if h == 2:
                    pool.wait_ge(unit_used, U_WO)
                    pool.dma_start(memn[:, :, :], mem[0].rearrange("(b p) d -> p b d", p=P)).then_inc(mem_in, 16)
            for n in (2, 3):
                pool.wait_ge(ln_done, NB * n)
                load_gb(n)

        @block.tensor
        def _(pe):
            mm = nc.tensor.matmul

            def need(u, i=None):
                pe.wait_ge(lo_done, lin(u + 1, SPL, i))

            def three(dst, lh, ll, rh, rl, start, stop):
                mm(dst, lh, rh, start=start, stop=False)
                mm(dst, lh, rl, start=False, stop=False)
                return mm(dst, ll, rh, start=False, stop=stop)

            def cols_part(u, dst, xh, xl, k0, k1):
                s = u % SPL
                for k in range(k0, k1):
                    last = three(dst, whi[s][:, k * P:(k + 1) * P], wlo[s][:, k * P:(k + 1) * P],
                                 xh[:, k, :], xl[:, k, :], k == 0, k == KT - 1)
                if k1 == KT:
                    last.then_inc(unit_used, 1)

            def transpose_rows(n, b):
                if n == 0:
                    pe.wait_ge(x_in[b], 16)
                else:
                    pe.wait_ge(ln_done, NB * (n - 1) + b + 1)
                for k in range(KT):
                    last = nc.tensor.transpose(ps[2 * b + k // 4][:, (k % 4) * P:(k % 4 + 1) * P],
                                               xn[:, b, k * P:(k + 1) * P], ident[:, :])
                last.then_inc(xtr_done, 1)

            def ffn_up(n):
                u0, xh, xl = U_FFN[n], xth[3 * n], xtl[3 * n]

                def tile(f, i=None):
                    bank = 2 * (f % 3)
                    if i is not None or n or f >= 3:
                        pe.wait_ge(h_done, lin(FT * n + f - 2, 3, i))
                    need(u0 + 2 * f, i)
                    cols_part(u0 + 2 * f, ps[bank][:, :], xh, xl, 0, KT)
                    need(u0 + 2 * f + 1, i)
                    cols_part(u0 + 2 * f + 1, ps[bank + 1][:, :], xh, xl, 0, KT)

                pe.wait_ge(xlo_done, NB * (3 * n + 1))
                if n == 0:
                    for f in range(3):
                        tile(f)
                with pe.Fori(1 - n, FT // 3) as i:
                    for f in range(3):
                        tile(f, i)
                tile(FT - 1)

            def down(n, order, first):
                u0, nk, h0 = DOWN[n]

                def product(k, b, start, stop):
                    u, s = u0 + k, (h0 + k) % SPL
                    for half in range(2):
                        c = slice(half * 512, half * 512 + 512)
                        last = three(ps[2 * b + half][:, :], hhi[s][:, b * P:(b + 1) * P],
                                     hlo[s][:, b * P:(b + 1) * P], whi[u % SPL][:, c], wlo[u % SPL][:, c],
                                     start, stop)
                    return last

                def k_tile(k, i=None):
                    need(u0 + k, i)
                    pe.wait_ge(hlo_done, lin(h0 + k + 1, SPL, i))
                    opening = k == 0 and i is None
                    for b in order:
                        if opening:
                            first(b)
                        last = product(k, b, opening, False)
                    last.then_inc(unit_used, 1)

                for k in range(min(nk - TAIL, SPL)):
                    k_tile(k)
                if nk - TAIL > SPL:
                    with pe.Fori(1, (nk - TAIL) // SPL) as i:
                        for k in range(SPL):
                            k_tile(k, i)
                for b in range(NB):
                    for k in range(nk - TAIL, nk):
                        if b == 0:
                            need(u0 + k)
                            pe.wait_ge(hlo_done, h0 + k + 1)
                        last = product(k, b, False, k == nk - 1)
                        if b == NB - 1:
                            last.then_inc(unit_used, 1)
                    if b < NB - 1:
                        last.then_inc(acc_done, 1)
                    if n < 3 and b >= 1:
                        transpose_rows(n + 1, b - 1)

            def rows_block(u0, b, dst, xh, xl):
                for t in range(4):
                    if b == 0:
                        need(u0 + t)
                    s = (u0 + t) % SPL
                    for kk in range(2):
                        k = 2 * t + kk
                        last = three(dst, xh[:, k, b * P:(b + 1) * P], xl[:, k, b * P:(b + 1) * P],
                                     whi[s][:, kk * 512:(kk + 1) * 512], wlo[s][:, kk * 512:(kk + 1) * 512],
                                     k == 0, k == KT - 1)
                    if b == NB - 1:
                        last.then_inc(unit_used, 1)
                if b < NB - 1:
                    last.then_inc(grp_done, 1)

            pe.wait_ge(small_in, 16 * 9)
            pe.wait_ge(pool_ok, 2)
            mm(ps[6][0:AH, :], relb[:, :], oh_sb[:, 0:512], start=True, stop=True)
            mm(ps[7][0:AH, 0:DIST - 512], relb[:, :], oh_sb[:, 512:DIST], start=True, stop=True)
            nc.tensor.transpose(ps[7][:, 256:256 + CK * KT + KT], crow[:, :],
                                ident[0:CK * KT + KT, 0:CK * KT + KT]).then_inc(brow_ready, 1)
            for b in range(NB):
                if b == 3:
                    pe.wait_ge(brow_done, 1)
                transpose_rows(0, b)

            ffn_up(0)
            down(0, (3, 1, 2, 0), lambda b: pe.wait_ge(h_done, {3: 1, 1: FT - 2, 2: FT - 1, 0: FT}[b]))

            xh, xl = xth[1], xtl[1]
            for b in range(NB):
                if b == 2:
                    transpose_rows(1, 3)
                pe.wait_ge(xlo_done, NB + b + 1)
                rows_block(U_VA, b, ps[2 * b][:, :], xh, xl)
            pe.wait_ge(wg_done, 1)
            for b in range(NB):
                for k in range(KT):
                    last = three(ps[1][:, b * 2 * MH:(b + 1) * 2 * MH], xh[:, k, b * P:(b + 1) * P],
                                 xl[:, k, b * P:(b + 1) * P], wg_hi[:, k, :], wg_lo[:, k, :], k == 0, k == KT - 1)
            last.then_inc(gate_mm, 1)

            def project(u, g, k0=0, k1=KT):
                if k0 == 0:
                    need(u)
                    pe.wait_ge(pj_ev, g if g == G_QK else g - 1)
                cols_part(u, ps[6 + g % 2][:, :], xh, xl, k0, k1)

            project(U_QK, G_QK)
            pe.wait_ge(gate_ev, 1)
            for b in range(NB):
                nc.tensor.transpose(ps[3][0:MH, b * P:(b + 1) * P], gates[:, b, 0:MH], ident[:, :])
                last = nc.tensor.transpose(ps[5][0:MH, b * P:(b + 1) * P], gates[:, b, MH:2 * MH], ident[:, :])
            last.then_inc(grow_ready, 1)
            project(U_QK + 1, G_QK + 1)
            pe.wait_ge(rows_done, 1)
            for c in range(NB):
                nc.tensor.transpose(ps[1][:, c * MH:(c + 1) * MH], r_a[:, c * P:(c + 1) * P], ident[0:MH, 0:MH])
                last = nc.tensor.transpose(ps[1][:, 16 + c * MH:16 + (c + 1) * MH], r_f[:, c * P:(c + 1) * P],
                                           ident[0:MH, 0:MH])
            last.then_inc(gcol_ready, 1)

            def logits(n):
                h, i = divmod(n, NB)
                p = h // 2
                if n % (2 * NB) == 0:
                    pe.wait_ge(pj_ev, G_QK + 2 * p + 2)
                if n == 1:
                    pe.wait_ge(acol_done, 1)
                    pe.wait_ge(emin_done, 1)
                if n >= 2:
                    pe.wait_ge(lg_done, n - 1)
                rows = slice((h % 2) * HD, (h % 2) * HD + HD)
                mm(ps[n % 2][:, 0:(i + 1) * P], qk[(2 * p) % 4][rows, i * P:(i + 1) * P],
                   qk[(2 * p + 1) % 4][rows, 0:(i + 1) * P], start=True, stop=True).then_inc(lg_ready, 1)

            def transpose_p(n):
                pe.wait_ge(p_done, n + 1)
                if n >= 2:
                    pe.wait_ge(pt_done, n - 1)
                if n >= 11 and n % 8 == 3:
                    pe.wait_ge(mt_ev, (n - 11) // 8 + 1)
                for j in range(n % NB + 1):
                    last = nc.tensor.transpose(ps[2 + n % 2][:, j * P:(j + 1) * P],
                                               lg[n % 3][:, j * P:(j + 1) * P], ident[:, :])
                last.then_inc(tr_done, 1)

            def values(n):
                h, i = divmod(n, NB)
                pe.wait_ge(pt_done, n + 1)
                if n >= 2:
                    pe.wait_ge(o_done, n - 1)
                for j in range(i + 1):
                    last = mm(ps[4 + n % 2][:, 0:HD], pt[n % PTS][:, j * P:(j + 1) * P],
                              va[:, j, h * HD:(h + 1) * HD], start=j == 0, stop=j == i)
                last.then_inc(pv_done, 1)

            def transpose_o(t):
                if t < PAIRS:
                    pe.wait_ge(o_done, 2 * NB * (t + 1))
                    pe.wait_ge(pt_done, min(8 * t + 10, NA))
                else:
                    pe.wait_ge(hn_done, t - PAIRS + 1)
                pe.wait_ge(mt_ev, t) if t else None
                for i in range(NB):
                    last = nc.tensor.transpose(ps[3][:, i * P:(i + 1) * P], ob[t % 2][:, i, :], ident[:, :])
                last.then_inc(ot_done, 1)

            def attention(n):
                if 2 <= n < NA + 2:
                    transpose_p(n - 2)
                if 3 <= n < NA + 3:
                    values(n - 3)
                if n < NA:
                    logits(n)

            for n in range(NA):
                attention(n)
                if n % 8 == 4 and n >= 12:
                    transpose_o((n - 12) // 8)
                q = 2 + n // 4
                project(U_QK + q, G_QK + q, 2 * (n % 4), 2 * (n % 4) + 2)

            def rows_group(u0, g, b):
                pe.wait_ge(pj_ev, g + b - 1)
                rows_block(u0, b, ps[6 + (g + b) % 2][:, :], xh, xl)

            for b in range(3):
                attention(NA + b)
                rows_group(U_VM, G_VM, b)
            transpose_o(PAIRS - 1)
            rows_group(U_VM, G_VM, 3)
            project(U_C1, G_C1)
            project(U_C1 + 1, G_C1 + 1)
            for b in range(NB):
                rows_group(U_OM, G_OM, b)

            def kq(h, j):
                s = NB * h + j
                if j == 0:
                    pe.wait_ge(conv_out, 2 * h + 2)
                if s < 2:
                    pe.wait_ge(lg_done, NA)
                else:
                    pe.wait_ge(st_done, s - 1)
                mm(ps[j % 2][:, 0:S - j * P], qk[(2 * h + 1) % 4][:, j * P:(j + 1) * P],
                   qk[(2 * h) % 4][:, j * P:S], start=True, stop=True).then_inc(kq_done, 1)

            def numerators(h):
                pe.wait_ge(st_done, NB * (h + 1))
                if h == 0:
                    pe.wait_ge(pj_ev, G_VM + NB)
                    pe.wait_ge(pool_ok, 3)
                    pe.wait_ge(o_done, NA)
                else:
                    pe.wait_ge(fin1_done, h)
                for i in range(NB):
                    c = 256 * (i % 2)
                    for j in range(i + 1):
                        slot = (NA + NB * h + j) % PTS
                        last = mm(ps[4 + i // 2][:, c:c + P + 1], pt[slot][:, (i - j) * P:(i - j + 1) * P],
                                  vx[:, j, h, :], start=j == 0, stop=j == i)
                last.then_inc(mpv_done, 1)

            for h in range(MH):
                if h == 0:
                    pe.wait_ge(pt_done, NA)
                else:
                    pe.wait_ge(e_done, NB * h)
                mm(ps[2][:, :], sel[:, h, :], grow[:, :], start=True, stop=True).then_inc(gb_ready, 1)
                kq(h, 0)
                kq(h, 1)
                if h < 2:
                    project(U_C2 + 2 * h, G_C2 + 2 * h)
                kq(h, 2)
                kq(h, 3)
                if h < 2:
                    project(U_C2 + 2 * h + 1, G_C2 + 2 * h + 1)
                if h:
                    transpose_o(PAIRS + h - 1)
                numerators(h)

            pe.wait_ge(mem_in, 16)
            for b in range(MB):
                if b == 0:
                    pe.wait_ge(pj_ev, G_C2 + 4)
                else:
                    pe.wait_ge(st_done, NB * MH)
                for k in range(KT):
                    last = nc.tensor.transpose(ps[(6 if b == 0 else 0) + k // 4][:, (k % 4) * P:(k % 4 + 1) * P],
                                               memn[:, b, k * P:(k + 1) * P], ident[:, :])
                last.then_inc(mtr_done, 1)
            transpose_o(KT - 1)

            def first(b):
                if b == 3:
                    pe.wait_ge(mlo_done, 1)
                elif b == 2:
                    pe.wait_ge(fin1_done, MH)
                elif b == 0:
                    pe.wait_ge(mlo_done, 2)
                else:
                    pe.wait_ge(mt_ev, KT)
            down(1, (3, 2, 0, 1), first)

            pe.wait_ge(xlo_done, NB * 2 + 2)
            for k in range(KT):
                if k == 3:
                    transpose_rows(2, 3)
                u = U_XV + k
                need(u)
                for b in range(MB):
                    for half in range(2):
                        c = slice(half * 512, half * 512 + 512)
                        last = three(ps[2 * b + half][:, :], mth[:, k, b * P:(b + 1) * P],
                                     mtl[:, k, b * P:(b + 1) * P], whi[u % SPL][:, c], wlo[u % SPL][:, c],
                                     k == 0, k == KT - 1)
                last.then_inc(unit_used, 1)
            for t in range(KT):
                if t == 0:
                    pe.wait_ge(xlo_done, NB * 2 + 3)
                elif t >= 2:
                    pe.wait_ge(xk_ev, t - 1)
                need(U_XK + t)
                cols_part(U_XK + t, ps[4 + t % 2][:, 0:MB * P], mth, mtl, 0, KT)

            def query(t, k0=0, k1=KT):
                if k0 == 0:
                    if t >= 2:
                        pe.wait_ge(xq_ev, t - 1)
                    need(U_XQ + t)
                cols_part(U_XQ + t, ps[6 + t % 2][:, :], xth[2], xtl[2], k0, k1)

            pe.wait_ge(xlo_done, NB * 3)
            query(0)
            query(1)
            for n in range(NX + 3):
                if 2 <= n < NX + 2:
                    m = n - 2
                    pe.wait_ge(xp_done, m + 1)
                    if m >= 2:
                        pe.wait_ge(xt_ev, m - 1)
                    for b in range(MB):
                        last = nc.tensor.transpose(ps[2 + m % 2][:, b * P:(b + 1) * P],
                                                   xp[m % 3][:, b * P:(b + 1) * P], ident[:, :])
                    last.then_inc(xt_done, 1)
                if n >= 6 and (n - 6) % NB == 0:
                    h = (n - 6) // NB
                    pe.wait_ge(xt_ev, NB * (h + 1))
                    if h:
                        pe.wait_ge(mt_ev, KT + 2 * h)
                    for c in range(2):
                        for b in range(MB):
                            last = mm(ps[4 + c][:, :], vmem[:, b, (2 * h + c) * P:(2 * h + c + 1) * P],
                                      xpt[h % 2][:, b, :], start=b == 0, stop=b == MB - 1)
                        last.then_inc(xo_ready, 1)
                if n < NX:
                    h, i = divmod(n, NB)
                    if i == 0:
                        pe.wait_ge(xq_ev, 2 * h + 2)
                    if n == 0:
                        pe.wait_ge(xk_ev, KT)
                        pe.wait_ge(xv_ev, 2 * MB)
                    if n >= 2:
                        pe.wait_ge(xe_done, n - 1)
                    for c in range(2):
                        last = mm(ps[n % 2][:, 0:MB * P], qx[(2 * h + c) % 4][:, i * P:(i + 1) * P],
                                  km[:, 2 * h + c, :], start=c == 0, stop=c == 1)
                    last.then_inc(xl_ready, 1)
                    if h < XH - 1:
                        query(2 * h + 2 + i // 2, 4 * (i % 2), 4 * (i % 2) + 4)

            def first(b):
                pe.wait_ge(*[(xe_done, NX), (xt_ev, NX), (mt_ev, 2 * KT), (xq_ev, KT)][b])
            down(2, (3, 0, 1, 2), first)
            transpose_rows(3, 3)

            ffn_up(1)
            down(3, (3, 1, 2, 0), lambda b: pe.wait_ge(h_done, {3: 1, 1: 2 * FT - 2, 2: 2 * FT - 1, 0: 2 * FT}[b]))

        @block.scalar
        def _(act):
            act.preload_act_table_set("natural_log_exp_and_others")
            step = Steps(act, a_step)

            def fn(*a, **k):
                return nc.scalar.activation(*a, **k)

            def split(c, i=None):
                if c >= U_END:
                    return
                act.wait_ge(raw_in[c % RAW], lin(16 * (c // RAW + 1), 16 * SPL // RAW, i))
                if i is not None or c >= SPL:
                    act.wait_ge(unit_used, lin(c - SPL + 1, SPL, i))
                fn(whi[c % SPL][:, :], raw[c % RAW][:, :], ACT.Copy).then_inc(hi_done, 1)

            def split_act(n, k, src, i=None):
                u0, nk, h0 = DOWN[n]
                if i is not None or k >= SPL:
                    act.wait_ge(unit_used, lin(u0 + k - SPL + 1, SPL, i))
                fn(hhi[(h0 + k) % SPL][:, :], src, ACT.Copy).then_inc(hhi_done, 1)

            def x_hi(n, b):
                act.wait_ge(xtr_done, NB * n + b + 1)
                for h in range(2):
                    last = fn(xth[n][:, 4 * h:4 * h + 4, b * P:(b + 1) * P],
                              ps[2 * b + h][:, :].rearrange("p (k c) -> p k c", k=4), ACT.Copy)
                last.then_inc(xhi_done, 1)

            def inv_std(n, b):
                act.wait_ge(var_done, NB * n + b + 1)
                step.link(fn(rstd[:, b:b + 1], mv[:, b, 1:2], ACT.Ln, bias=eps_col[:, 0:1]))
                fn(rstd[:, b:b + 1], rstd[:, b:b + 1], ACT.Exp, scale=-0.5).then_inc(rstd_done, 1)

            def h_tile(n, k, i=None):
                if i is None:
                    return hb[n][:, k * S:(k + 1) * S]
                return hb[n][:, bass.ds(k * S + i * (SPL * S), S)]

            def split_h(n, k, i=None):
                act.wait_ge(h_done, lin(FT * n + k + 1, SPL, i))
                split_act(3 * n, k, h_tile(n, k, i), i)

            def split_mt(n, k):
                act.wait_ge(mt_ev, KT * (n - 1) + k + 1)
                split_act(n, k, mt[:, k * S:(k + 1) * S])

            def ffn_up(n):
                u0 = U_FFN[n]

                def tile(f, i=None):
                    split(u0 + 2 * f + AHEAD, i)
                    act.wait_ge(unit_used, lin(u0 + 2 * f + 1, SPL, i))
                    if i is not None or n or f >= 3:
                        act.wait_ge(h_done, lin(FT * n + f - 2, 3, i))
                    fn(eg[n][f % 3][:, :], ps[2 * (f % 3)][:, :], ACT.Exp, scale=-1.0).then_inc(eg_ready, 1)
                    split(u0 + 2 * f + AHEAD + 1, i)

                if n == 0:
                    for f in range(3):
                        tile(f)
                with act.Fori(1 - n, FT // 3) as i:
                    for f in range(3):
                        tile(f, i)
                if n == 0:
                    act.wait_ge(scr_out, 16)
                for k in range(3):
                    split_h(n, k)
                tile(FT - 1)

            def ffn_down(n):
                u0 = DOWN[3 * n][0]
                with act.Fori(0, (FT - TAIL) // SPL) as i:
                    for k in range(SPL):
                        split(u0 + k + AHEAD, i)
                        split_h(n, k + 3, i)
                split_h(n, FT - 1)
                tail(3 * n)

            def mt_down(n):
                for k in range(KT - TAIL):
                    split(DOWN[n][0] + k + AHEAD)
                    split_mt(n, k + 3)
                split_mt(n, KT - 1)
                tail(n)

            def tail(n):
                ut = DOWN[n][0] + DOWN[n][1] - TAIL
                split(ut + AHEAD)
                inv_std(n, 0)
                split(ut + AHEAD + 1)
                inv_std(n, 1)
                if n < 3:
                    x_hi(n + 1, 0)
                inv_std(n, 2)
                if n < 3:
                    x_hi(n + 1, 1)
                split(ut + AHEAD + 2)
                split(ut + AHEAD + 3)
                inv_std(n, 3)
                if n < 3:
                    x_hi(n + 1, 2)

            act.wait_ge(pool_ok, 3)
            act.wait_ge(small_in, 16 * 9)
            fn(wg_hi[:, :, :], wg_raw[:, :, :], ACT.Copy).then_inc(wg_hi_done, 1)
            for b in range(NB):
                x_hi(0, b)
                split(b)
            ffn_up(0)
            ffn_down(0)

            def evacuate(g, dst, ready, value, func=ACT.Copy, scale=1.0, bank=None):
                act.wait_ge(ready, value)
                src = ps[6 + g % 2 if bank is None else bank][:, :]
                if len(dst.shape) == 3:
                    src = src.rearrange("p (h c) -> p h c", h=dst.shape[1])
                fn(dst, src, func, scale=scale).then_inc(pj_ev, 1)

            def va_block(b):
                ready = (grp_done, b + 1) if b < 3 else (unit_used, U_VA + 4)
                evacuate(b, va[:, b, :], *ready, bank=2 * b)

            split(U_VA + 4)
            va_block(0)
            split(U_VA + 5)
            va_block(1)
            x_hi(1, 3)
            va_block(2)
            split(U_VA + 6)
            split(U_VA + 7)
            va_block(3)
            act.wait_ge(gate_mm, 1)
            fn(gates[:, :, :], ps[1][:, 0:NB * 2 * MH].rearrange("p (b c) -> p b c", b=NB), ACT.Copy)\
                .then_inc(gate_ev, 1)

            def qk_tile(t):
                evacuate(G_QK + t, qk[t % 4][:, :], unit_used, U_QK + t + 1)

            def conv_tile(t):
                if t >= 2:
                    act.wait_ge(conv_out, t - 1)
                evacuate(G_CONV[t], craw[t % 2][:, CK - 1:], unit_used, U_CONV[t] + 1)

            def conv_exp(t):
                act.wait_ge(conv_y, t + 1)
                fn(craw[t % 2][:, CK - 1:], cy[t % 2][:, :], ACT.Exp, scale=-1.0).then_inc(conv_e, 1)

            split(U_QK + 4)
            qk_tile(0)
            act.wait_ge(fabs_done, 1)
            step.link(fn(r_e[:, :], r_e[:, :], ACT.Exp, scale=-1.0))
            fn(r_e[:, :], r_e[:, :], ACT.Ln, bias=1.0).then_inc(flog_done, 1)
            split(U_QK + 5)
            qk_tile(1)
            act.wait_ge(gcol_ready, 1)
            act.wait_ge(acol_done, 1)
            fn(emin[:, :, :], ps[1][:, 16:32].rearrange("p (b c) -> p b c", b=NB), ACT.Exp).then_inc(emin_done, 1)

            def probs(n):
                w = (n % NB + 1) * P
                act.wait_ge(nmax_done, n + 1)
                fn(lg[n % 3][:, 0:w], lg[n % 3][:, 0:w], ACT.Exp, bias=nmax[:, n:n + 1],
                   accum_out=rsum[:, n:n + 1]).then_inc(p_done, 1)

            def p_copy(n):
                w = (n % NB + 1) * P
                act.wait_ge(tr_done, n + 1)
                if n >= PTS:
                    act.wait_ge(pv_done, n - PTS + 1)
                fn(pt[n % PTS][:, 0:w], ps[2 + n % 2][:, 0:w], ACT.Copy).then_inc(pt_done, 1)

            def mt_copy(t):
                act.wait_ge(ot_done, t + 1)
                fn(mt[:, t * S:(t + 1) * S], ps[3][:, :], ACT.Copy).then_inc(mt_ev, 1)

            for n in range(NA):
                if n % 4 == 0:
                    split(U_QK + 2 + n // 4 + AHEAD)
                    t = 1 + n // 4
                    if 2 <= t < 2 * PAIRS:
                        qk_tile(t)
                    elif t >= 2:
                        conv_tile(t - 2 * PAIRS)
                probs(n)
                if n >= 2:
                    p_copy(n - 2)
                if n % 8 == 4 and n >= 12:
                    mt_copy((n - 12) // 8)
            conv_exp(0)
            conv_tile(1)
            p_copy(NA - 2)
            split(U_VM + 4)

            def vm_block(b):
                ready = (grp_done, 3 + b + 1) if b < 3 else (unit_used, U_VM + 4)
                evacuate(G_VM + b, vx[:, b, :, 0:P], *ready)

            def om_block(b):
                ready = (grp_done, 6 + b + 1) if b < 3 else (unit_used, U_OM + 4)
                evacuate(G_OM + b, om[:, b, :], *ready, func=ACT.Exp, scale=-1.0)

            vm_block(0)
            p_copy(NA - 1)
            split(U_VM + 5)
            vm_block(1)
            conv_exp(1)
            vm_block(2)
            mt_copy(PAIRS - 1)
            split(U_VM + 6)
            split(U_VM + 7)
            vm_block(3)
            split(U_C1 + AHEAD)
            conv_tile(2)
            split(U_C1 + 1 + AHEAD)
            conv_tile(3)
            conv_exp(2)
            split(U_OM + 4)
            om_block(0)
            split(U_OM + 5)
            conv_exp(3)
            om_block(1)
            om_block(2)
            split(U_OM + 6)
            split(U_OM + 7)
            om_block(3)

            def weights(h, j):
                s = NB * h + j
                if j == 0:
                    act.wait_ge(gb_ready, h + 1)
                if s == 0:
                    act.wait_ge(acol_done, 1)
                if s >= 2:
                    act.wait_ge(st_done, s - 1)
                fn(ew[j % 2][:, 0:S - j * P], ps[2][:, j * P:S], ACT.Exp, scale=-1.0,
                   bias=acol[:, j, h:h + 1]).then_inc(e_done, 1)

            def head_std(h):
                act.wait_ge(hvar_done, h + 1)
                step.link(fn(hrs[:, :], hmv[:, :, 1], ACT.Ln, bias=eps_col[:, 0:1]))
                fn(hrs[:, :], hrs[:, :], ACT.Exp, scale=-0.5).then_inc(hr_done, 1)

            for h in range(MH):
                weights(h, 0)
                weights(h, 1)
                if h:
                    head_std(h - 1)
                if h < 2:
                    split(U_C2 + 2 * h + AHEAD)
                    conv_tile(4 + 2 * h)
                weights(h, 2)
                weights(h, 3)
                if h < 2:
                    split(U_C2 + 2 * h + 1 + AHEAD)
                    conv_tile(5 + 2 * h)
                if h == MH - 1:
                    for k in range(3):
                        split_mt(1, k)
                if h:
                    mt_copy(PAIRS + h - 1)
                if h < 2:
                    conv_exp(4 + 2 * h)
                    conv_exp(5 + 2 * h)

            def mem_hi(b):
                act.wait_ge(mtr_done, b + 1)
                for h in range(2):
                    last = fn(mth[:, 4 * h:4 * h + 4, b * P:(b + 1) * P],
                              ps[(6 if b == 0 else 0) + h][:, :].rearrange("p (k c) -> p k c", k=4), ACT.Copy)
                last.then_inc(mhi_done, 1)

            mem_hi(0)
            head_std(MH - 1)
            mem_hi(1)
            mt_copy(KT - 1)
            mt_down(1)

            for k in range(KT):
                split(U_XV + k + AHEAD)
                if k == 3:
                    x_hi(2, 3)
            act.wait_ge(unit_used, U_XV + KT)
            for b in range(MB):
                for h in range(2):
                    fn(vmem[:, b, h * 512:(h + 1) * 512], ps[2 * b + h][:, :], ACT.Copy).then_inc(xv_ev, 1)
            for t in range(KT):
                split(U_XK + t + AHEAD)
                act.wait_ge(unit_used, U_XK + t + 1)
                fn(km[:, t, :], ps[4 + t % 2][:, 0:MB * P], ACT.Copy).then_inc(xk_ev, 1)

            def query(t):
                act.wait_ge(unit_used, U_XQ + t + 1)
                fn(qx[t % 4][:, :], ps[6 + t % 2][:, :], ACT.Copy, scale=XSCALE).then_inc(xq_ev, 1)

            split(U_XQ + AHEAD)
            query(0)
            split(U_XQ + 1 + AHEAD)
            query(1)
            for n in range(NX + 4):
                if n % 2 == 0 and n < 12:
                    split(U_XQ + 2 + n // 2 + AHEAD)
                if n % 2 == 0 and 2 <= n <= 12:
                    query(1 + n // 2)
                if n < NX:
                    act.wait_ge(xm_done, n + 1)
                    if n >= 3:
                        act.wait_ge(xt_done, n - 2)
                    fn(xp[n % 3][:, :], ps[n % 2][:, 0:MB * P], ACT.Exp, bias=nmax[:, n:n + 1],
                       accum_out=rsum[:, n:n + 1]).then_inc(xe_done, 1)
                if 2 <= n < NX + 2:
                    h, i = divmod(n - 2, NB)
                    act.wait_ge(xt_done, n - 1)
                    if h >= 2:
                        act.wait_ge(xo_ready, 2 * (h - 1))
                    fn(xpt[h % 2][:, :, i * P:(i + 1) * P],
                       ps[2 + n % 2][:, 0:MB * P].rearrange("p (b c) -> p b c", b=MB), ACT.Copy).then_inc(xt_ev, 1)
                if n >= 7 and (n - 7) % NB == 0:
                    h = (n - 7) // NB
                    for c in range(2):
                        act.wait_ge(xo_ready, 2 * h + c + 1)
                        t = 2 * h + c
                        fn(mt[:, t * S:(t + 1) * S], ps[4 + c][:, :], ACT.Copy).then_inc(mt_ev, 1)
                if n == NX - 1:
                    for k in range(3):
                        split_mt(2, k)
            mt_down(2)
            x_hi(3, 3)
            ffn_up(1)
            ffn_down(1)

        @block.vector
        def _(dve):
            v = nc.vector
            step = Steps(dve, v_step)

            def split(c, i=None):
                if c >= U_END:
                    return
                dve.wait_ge(hi_done, lin(c + 1, SPL, i))
                v.tensor_tensor(wlo[c % SPL][:, :], raw[c % RAW][:, :], whi[c % SPL][:, :].bitcast(F32),
                                ALU.subtract).then_inc(lo_done, 1)

            def split_act(n, k, src, i=None):
                u0, nk, h0 = DOWN[n]
                s = (h0 + k) % SPL
                dve.wait_ge(hhi_done, lin(h0 + k + 1, SPL, i))
                v.tensor_tensor(hlo[s][:, :], src, hhi[s][:, :].bitcast(F32), ALU.subtract).then_inc(hlo_done, 1)

            def x_lo(n, b):
                dve.wait_ge(xhi_done, NB * n + b + 1)
                for h in range(2):
                    blk = (slice(None), slice(4 * h, 4 * h + 4), slice(b * P, (b + 1) * P))
                    last = v.tensor_tensor(xtl[n][blk], ps[2 * b + h][:, :].rearrange("p (k c) -> p k c", k=4),
                                           xth[n][blk].bitcast(F32), ALU.subtract)
                last.then_inc(xlo_done, 1)

            def norm(n, b):
                ut = DOWN[n][0] + DOWN[n][1]
                if b < NB - 1:
                    dve.wait_ge(acc_done, (NB - 1) * n + b + 1)
                else:
                    dve.wait_ge(unit_used, ut)
                for h in range(2):
                    half = xn[:, b, h * 512:(h + 1) * 512]
                    step.inc(v.scalar_tensor_tensor(out=half, in0=half, scalar=ALPHA, in1=ps[2 * b + h][:, :],
                                                    op0=ALU.mult, op1=ALU.add))
                dve.wait_ge(v_step, step.base + step.k)
                for h in range(2):
                    step.inc(v.bn_stats(stats[:, h, :], xn[:, b, h * 512:(h + 1) * 512]))
                dve.wait_ge(v_step, step.base + step.k)
                v.bn_aggr(mv[:, b, :], stats[:, :, :]).then_inc(var_done, 1)
                dve.wait_ge(gb_in, 32 * (n + 1))
                dve.wait_ge(var_done, NB * n + b + 1)
                step.link(v.scalar_tensor_tensor(out=xn[:, b, :], in0=xn[:, b, :], scalar=mv[:, b, 0:1],
                                                 in1=gb[:, 0, :], op0=ALU.subtract, op1=ALU.mult))
                dve.wait_ge(rstd_done, NB * n + b + 1)
                v.scalar_tensor_tensor(out=xn[:, b, :], in0=xn[:, b, :], scalar=rstd[:, b:b + 1],
                                       in1=gb[:, 1, :], op0=ALU.mult, op1=ALU.add).then_inc(ln_done, 1)

            def split_h(n, k, i=None):
                src = hb[n][:, k * S:(k + 1) * S] if i is None else hb[n][:, bass.ds(k * S + i * (SPL * S), S)]
                split_act(3 * n, k, src, i)

            def split_mt(n, k):
                split_act(n, k, mt[:, k * S:(k + 1) * S])

            def ffn_up(n):
                u0 = U_FFN[n]

                def tile(f, i=None):
                    split(u0 + 2 * f + AHEAD, i)
                    split(u0 + 2 * f + AHEAD + 1, i)
                    e, bank = eg[n][f % 3], 2 * (f % 3)
                    dve.wait_ge(eg_ready, lin(FT * n + f + 1, 3, i))
                    step.link(v.tensor_scalar(e[:, :], e[:, :], 1.0, None, ALU.add))
                    step.link(v.reciprocal(e[:, :], e[:, :]))
                    step.link(v.tensor_tensor(e[:, :], ps[bank][:, :], e[:, :], ALU.mult))
                    dve.wait_ge(unit_used, lin(u0 + 2 * f + 2, SPL, i))
                    dst = hb[n][:, f * S:(f + 1) * S] if i is None else hb[n][:, bass.ds(f * S + i * (3 * S), S)]
                    v.scalar_tensor_tensor(out=dst, in0=e[:, :], scalar=0.5, in1=ps[bank + 1][:, :],
                                           op0=ALU.mult, op1=ALU.mult).then_inc(h_done, 1)

                if n == 0:
                    for f in range(3):
                        tile(f)
                with dve.Fori(1 - n, FT // 3) as i:
                    step.enter(i if n else i - 1, 9)
                    for f in range(3):
                        tile(f, i)
                step.leave(FT // 3 - 1 + n, 9)
                for k in range(3):
                    split_h(n, k)
                tile(FT - 1)

            def ffn_down(n):
                u0 = DOWN[3 * n][0]
                with dve.Fori(0, (FT - TAIL) // SPL) as i:
                    for k in range(SPL):
                        split(u0 + k + AHEAD, i)
                        split_h(n, k + 3, i)
                split_h(n, FT - 1)
                tail(3 * n)

            def mt_down(n):
                for k in range(KT - TAIL):
                    split(DOWN[n][0] + k + AHEAD)
                    split_mt(n, k + 3)
                split_mt(n, KT - 1)
                tail(n)

            def tail(n):
                ut = DOWN[n][0] + DOWN[n][1] - TAIL
                split(ut + AHEAD)
                norm(n, 0)
                split(ut + AHEAD + 1)
                norm(n, 1)
                if n < 3:
                    x_lo(n + 1, 0)
                norm(n, 2)
                if n < 3:
                    x_lo(n + 1, 1)
                split(ut + AHEAD + 2)
                split(ut + AHEAD + 3)
                norm(n, 3)
                if n < 3:
                    x_lo(n + 1, 2)

            step.link(v.memset(eps_col[:, :], LN_EPS))
            dve.wait_ge(brow_ready, 1)
            step.inc(v.tensor_tensor(tb_sb[:, 0:512], ps[6][0:AH, :], lnm_sb[:, 0:512], ALU.add))
            step.inc(v.tensor_tensor(tb_sb[:, 512:DIST], ps[7][0:AH, 0:DIST - 512], lnm_sb[:, 512:DIST], ALU.add))
            dve.wait_ge(v_step, step.k)
            v.tensor_copy(ccol[:, :], ps[7][:, 256:256 + CK * KT + KT]).then_inc(brow_done, 1)
            dve.wait_ge(wg_hi_done, 1)
            v.tensor_tensor(wg_lo[:, :, :], wg_raw[:, :, :], wg_hi[:, :, :].bitcast(F32), ALU.subtract).then_inc(wg_done, 1)
            for b in range(NB):
                x_lo(0, b)
                split(b)
            ffn_up(0)
            ffn_down(0)

            split(U_VA + 4)
            split(U_VA + 5)
            x_lo(1, 3)
            split(U_VA + 6)
            split(U_VA + 7)
            for s in range(2):
                step.link(v.memset(craw[s][:, 0:CK - 1], 0.0))
            step.link(v.memset(r_one[:, :], 1.0))
            split(U_QK + 4)
            dve.wait_ge(grow_ready, 1)
            step.link(v.tensor_scalar(r_ig[:, :], ps[3][0:MH, :], gbias[:, 0:1], None, ALU.add))
            step.link(v.tensor_scalar(r_f[:, :], ps[5][0:MH, :], gbias[:, 1:2], None, ALU.add))
            v.scalar_tensor_tensor(out=r_e[:, :], in0=r_f[:, :], scalar=-1.0, in1=r_f[:, :],
                                   op0=ALU.mult, op1=ALU.max).then_inc(fabs_done, 1)
            dve.wait_ge(flog_done, 1)
            step.link(v.scalar_tensor_tensor(out=r_f[:, :], in0=r_f[:, :], scalar=0.0, in1=r_e[:, :],
                                             op0=ALU.min, op1=ALU.subtract))
            step.link(v.tensor_tensor_scan(r_sum[:, :], r_one[:, :], r_f[:, :], 0.0, ALU.mult, ALU.add))
            step.link(v.tensor_tensor(r_a[:, :], r_ig[:, :], r_sum[:, :], ALU.subtract))
            step.link(v.tensor_tensor_scan(grow[:, :], r_a[:, :], r_a[:, :], 0.0, ALU.max, ALU.max))
            v.scalar_tensor_tensor(out=r_f[:, :], in0=r_sum[:, :], scalar=-1.0, in1=grow[:, :],
                                   op0=ALU.mult, op1=ALU.subtract).then_inc(rows_done, 1)
            split(U_QK + 5)
            dve.wait_ge(gcol_ready, 1)
            v.tensor_copy(acol[:, :, :], ps[1][:, 0:16].rearrange("p (b c) -> p b c", b=NB)).then_inc(acol_done, 1)

            def logits(n):
                h, i = divmod(n, NB)
                w = (i + 1) * P
                dve.wait_ge(lg_ready, n + 1)
                if i == 0:
                    dve.wait_ge(wb_in[h % 2], 16 * (h // 2 + 1))
                if n >= 3:
                    dve.wait_ge(tr_done, n - 2)
                v.scalar_tensor_tensor(out=lg[n % 3][:, 0:w], in0=ps[n % 2][:, 0:w], scalar=HD ** -0.5,
                                       in1=wb[h % 2][:, S - w:S], op0=ALU.mult, op1=ALU.add).then_inc(lg_done, 1)
                dve.wait_ge(lg_done, n + 1)
                v.tensor_reduce(nmax[:, n:n + 1], lg[n % 3][:, 0:w], AXX, ALU.max, negate=True).then_inc(nmax_done, 1)

            def divide(n):
                h, i = divmod(n, NB)
                p = h // 2
                dve.wait_ge(pv_done, n + 1)
                if n % 8 == 0 and p >= 2:
                    dve.wait_ge(ot_done, p - 1)
                step.link(v.reciprocal(rinv[:, n:n + 1], rsum[:, n:n + 1]))
                v.tensor_scalar(ob[p % 2][:, i, (h % 2) * HD:(h % 2 + 1) * HD], ps[4 + n % 2][:, 0:HD],
                                rinv[:, n:n + 1], None, ALU.mult).then_inc(o_done, 1)

            def conv(t):
                c = t // 2 + MH * (t % 2)
                y, r = cy[t % 2], craw[t % 2]
                dve.wait_ge(pj_ev, G_CONV[t] + 1)
                step.link(v.tensor_scalar(y[:, :], r[:, 0:S], ccol[:, c:c + 1],
                                          ccol[:, CK * KT + c:CK * KT + c + 1], ALU.mult, ALU.add))
                for j in range(1, CK):
                    last = v.scalar_tensor_tensor(out=y[:, :], in0=r[:, j:j + S], scalar=ccol[:, KT * j + c:KT * j + c + 1],
                                                  in1=y[:, :], op0=ALU.mult, op1=ALU.add)
                    if j < CK - 1:
                        step.link(last)
                last.then_inc(conv_y, 1)

            def silu(t):
                y, e = cy[t % 2], craw[t % 2][:, CK - 1:]
                dve.wait_ge(conv_e, t + 1)
                step.link(v.tensor_scalar(e, e, 1.0, None, ALU.add))
                step.link(v.reciprocal(e, e))
                if t >= 4:
                    dve.wait_ge(kq_done, NB * (t // 2 - 1))
                v.tensor_tensor(qk[t % 4][:, :], y[:, :], e, ALU.mult).then_inc(conv_out, 1)

            for n in range(NA):
                if n % 4 == 0:
                    split(U_QK + 2 + n // 4 + AHEAD)
                logits(n)
                if n >= 3:
                    divide(n - 3)
                if n == 29:
                    conv(0)
            divide(NA - 3)
            silu(0)
            conv(1)
            split(U_VM + 4)
            divide(NA - 2)
            split(U_VM + 5)
            divide(NA - 1)
            silu(1)
            split(U_VM + 6)
            split(U_VM + 7)
            split(U_C1 + AHEAD)
            conv(2)
            split(U_C1 + 1 + AHEAD)
            conv(3)
            silu(2)

            def sigmoid_om(b):
                dve.wait_ge(pj_ev, G_OM + b + 1)
                step.link(v.tensor_scalar(om[:, b, :], om[:, b, :], 1.0, None, ALU.add))
                v.reciprocal(om[:, b, :], om[:, b, :]).then_inc(om_done, 1)

            split(U_OM + 4)
            sigmoid_om(0)
            split(U_OM + 5)
            silu(3)
            sigmoid_om(1)
            sigmoid_om(2)
            split(U_OM + 6)
            split(U_OM + 7)
            sigmoid_om(3)

            def weigh(h, j):
                s = NB * h + j
                w = S - j * P
                dve.wait_ge(kq_done, s + 1)
                dve.wait_ge(em_done, s + 1)
                if s < PTS:
                    dve.wait_ge(pv_done, NA + s - PTS + 1)
                else:
                    dve.wait_ge(mpv_done, (s - PTS) // NB + 1)
                v.scalar_tensor_tensor(out=pt[(NA + s) % PTS][:, 0:w], in0=ps[j % 2][:, 0:w], scalar=float(P) ** -0.5,
                                       in1=ew[j % 2][:, 0:w], op0=ALU.mult, op1=ALU.mult).then_inc(st_done, 1)

            def gated(h):
                dve.wait_ge(mpv_done, h + 1)
                if h == 0:
                    dve.wait_ge(emin_done, 1)
                    dve.wait_ge(om_done, NB)
                num = [ps[4 + c][:, :].rearrange("p (i c) -> p i c", i=2)[:, :, P] for c in range(2)]
                for c in range(2):
                    step.inc(v.scalar_tensor_tensor(out=den[:, 2 * c:2 * c + 2], in0=num[c], scalar=-1.0,
                                                    in1=emin[:, 2 * c:2 * c + 2, h], op0=ALU.mult, op1=ALU.max))
                dve.wait_ge(v_step, step.k + step.base)
                for c in range(2):
                    step.inc(v.tensor_tensor(den[:, 2 * c:2 * c + 2], num[c], den[:, 2 * c:2 * c + 2], ALU.max))
                dve.wait_ge(v_step, step.k + step.base)
                step.link(v.reciprocal(den[:, :], den[:, :]))
                dve.wait_ge(ot_done, h + 3)
                o = ob[h % 2]
                for i in range(NB):
                    last = v.scalar_tensor_tensor(out=o[:, i, :], in0=ps[4 + i // 2][:, 256 * (i % 2):256 * (i % 2) + P],
                                                  scalar=den[:, i:i + 1], in1=om[:, i, h * P:(h + 1) * P],
                                                  op0=ALU.mult, op1=ALU.mult)
                    if i < NB - 1:
                        step.inc(last)
                last.then_inc(fin1_done, 1)
                dve.wait_ge(v_step, step.k + step.base)
                dve.wait_ge(fin1_done, h + 1)
                for i in range(NB):
                    step.inc(v.bn_stats(hst[:, i, :], o[:, i, :]))
                dve.wait_ge(v_step, step.k + step.base)
                for i in range(NB):
                    last = v.bn_aggr(hmv[:, i, :], hst[:, i, :])
                    if i < NB - 1:
                        step.inc(last)
                last.then_inc(hvar_done, 1)

            def head_norm(h):
                o = ob[h % 2]
                dve.wait_ge(v_step, step.k + step.base)
                dve.wait_ge(hr_done, h + 1)
                for i in range(NB):
                    step.inc(v.tensor_scalar(o[:, i, :], o[:, i, :], hmv[:, i, 0:1], hrs[:, i:i + 1],
                                             ALU.subtract, ALU.mult))
                dve.wait_ge(v_step, step.k + step.base)
                gain = mlg[:, h * P:(h + 1) * P].unsqueeze(1).to_broadcast([P, NB, P])
                v.tensor_tensor(o[:, :, :], o[:, :, :], gain, ALU.mult).then_inc(hn_done, 1)

            for h in range(MH):
                weigh(h, 0)
                weigh(h, 1)
                if h:
                    gated(h - 1)
                if h < 2:
                    split(U_C2 + 2 * h + AHEAD)
                    conv(4 + 2 * h)
                weigh(h, 2)
                weigh(h, 3)
                if h:
                    head_norm(h - 1)
                if h < 2:
                    split(U_C2 + 2 * h + 1 + AHEAD)
                    conv(5 + 2 * h)
                    silu(4 + 2 * h)
                    silu(5 + 2 * h)
            for k in range(3):
                split_mt(1, k)

            def mem_lo(b):
                dve.wait_ge(mhi_done, b + 1)
                for h in range(2):
                    blk = (slice(None), slice(4 * h, 4 * h + 4), slice(b * P, (b + 1) * P))
                    src = ps[(6 if b == 0 else 0) + h][:, :].rearrange("p (k c) -> p k c", k=4)
                    last = v.tensor_tensor(mtl[blk], src, mth[blk].bitcast(F32), ALU.subtract)
                last.then_inc(mlo_done, 1)

            gated(MH - 1)
            mem_lo(0)
            head_norm(MH - 1)
            mem_lo(1)
            mt_down(1)

            for k in range(KT):
                split(U_XV + k + AHEAD)
                if k == 3:
                    x_lo(2, 3)
            for t in range(KT):
                split(U_XK + t + AHEAD)
            split(U_XQ + AHEAD)
            split(U_XQ + 1 + AHEAD)
            for n in range(NX + 1):
                if n % 2 == 0 and n < 12:
                    split(U_XQ + 2 + n // 2 + AHEAD)
                if n < NX:
                    dve.wait_ge(xl_ready, n + 1)
                    v.tensor_reduce(nmax[:, n:n + 1], ps[n % 2][:, 0:MB * P], AXX, ALU.max, negate=True)\
                        .then_inc(xm_done, 1)
                if n >= 1:
                    m = n - 1
                    dve.wait_ge(xe_done, m + 1)
                    step.link(v.reciprocal(rinv[:, m:m + 1], rsum[:, m:m + 1]))
                    v.tensor_scalar(xp[m % 3][:, :], xp[m % 3][:, :], rinv[:, m:m + 1], None, ALU.mult)\
                        .then_inc(xp_done, 1)
            for k in range(3):
                split_mt(2, k)
            mt_down(2)
            x_lo(3, 3)
            ffn_up(1)
            ffn_down(1)


def key_distance_tables(seq, buckets, max_dist, heads):
    import numpy as np
    d = seq - 1 - np.arange(seq + P)
    exact = buckets // 2
    df = np.maximum(d, 1).astype(np.float32)
    large = exact + (np.log(df / np.float32(exact)) / np.float32(math.log(max_dist / exact))
                     * np.float32(buckets - exact)).astype(np.int32)
    bucket = np.where(d < exact, np.maximum(d, 0), np.minimum(large, buckets - 1))
    onehot = (np.arange(buckets)[:, None] == bucket[None, :]).astype(np.float32)
    count = np.zeros(d.shape)
    for window, dilation in ((128, 1), (512, 4), (2048, 16)):
        count += (d >= 0) & (d % dilation == 0) & (d // dilation <= window // dilation)
    row = np.where(count > 0, np.log(np.maximum(count, 1)), -1e30).astype(np.float32)
    return onehot, np.ascontiguousarray(np.broadcast_to(row, (heads, d.size)))


_INS = ['x', 'mem', 'rel_bias', 'ln_g', 'ln_b', 'ffn_w_gate', 'ffn_w_up', 'ffn_w_down', 'w_in', 'conv_w', 'conv_b',
        'ig_bias', 'fg_bias', 'ml_norm_g', 'w_out', 'xq_w', 'xkv_w', 'xo_w']


def kernel(**inputs):
    import numpy as np
    import concourse.bacc as bacc
    from concourse.bass_utils import run_bass_kernel_spmd

    nc = bacc.Bacc("TRN2", target_bir_lowering=False, num_devices=1)
    arrays, args = {}, []
    onehot, lnm = key_distance_tables(inputs['x'].shape[1], inputs['rel_bias'].shape[0], 2048,
                                      inputs['rel_bias'].shape[1])
    named = [(n, np.ascontiguousarray(inputs[n])) for n in _INS] + [('onehot', onehot), ('lnm', lnm)]
    for name, a in named:
        arrays[f"in_{name}"] = a
        args.append(nc.dram_tensor(f"in_{name}", a.shape, mybir.dt.from_np(a.dtype), kind="ExternalInput").ap())
    args.append(nc.dram_tensor("bias_rows", (lnm.shape[0], P, lnm.shape[1]), F32).ap())
    args.append(nc.dram_tensor("out", inputs['x'].shape, F32, kind="ExternalOutput").ap())
    macaron_layer(nc, *args)
    r = run_bass_kernel_spmd(nc, [arrays], core_ids=[0])
    return r.results[0]["out"]
```

```python
import math
from contextlib import ExitStack

import concourse.bass as bass
from concourse import mybir

F32 = mybir.dt.float32
F32R = mybir.dt.float32r
ALU = mybir.AluOpType
ACT = mybir.ActivationFunctionType
AXX = mybir.AxisListType.X

P = 128
LN_EPS = 1e-5
ALPHA = 2 ** 0.25

RAW = 3
SPL = 6
AHEAD = 4
TAIL = 4
PTS = 5


def lin(const, per, i):
    return const if i is None else const + i * per


class Steps:

    def __init__(self, eng, sem):
        self.eng, self.sem, self.base, self.k = eng, sem, 0, 0

    def inc(self, ins):
        self.k += 1
        ins.then_inc(self.sem, 1)

    def link(self, ins):
        self.inc(ins)
        self.eng.wait_ge(self.sem, self.base + self.k)

    def enter(self, i, per):
        self.outer = self.base + self.k
        self.base, self.k = self.outer + i * per, 0

    def leave(self, rounds, per):
        assert self.k == per, (self.k, per)
        self.base, self.k = self.outer + rounds * per, 0


def macaron_layer(nc, x, mem, rel_bias, ln_g, ln_b, w_gate, w_up, w_down, w_in, conv_w, conv_b,
                  ig_bias, fg_bias, ml_g, w_out, xq_w, xkv_w, xo_w, onehot, lnm, bias_rows, g_rows, out):
    S, D = x.shape[1], x.shape[2]
    FF = w_gate.shape[3]
    KT = D // P
    NB = S // P
    MB = mem.shape[1] // P
    FT = FF // P
    AH = rel_bias.shape[1]
    AW = D // 2
    HD = AW // AH
    PAIRS = AH // 2
    MH = ig_bias.shape[1]
    MW = D // 2
    XH = 4
    XSCALE = (D // XH) ** -0.5
    CK = conv_w.shape[1]
    DIST = onehot.shape[1]
    GW = 32 + MH
    NA = AH * NB
    NX = XH * NB
    assert (S, D, MB, MW // MH, KT, HD, CK) == (512, 1024, 2, P, 8, 64, 4)
    assert FT % 3 == 1 and (FT - TAIL) % SPL == 0 and SPL == 2 * RAW

    U_VA = 3 * FT
    U_QK = U_VA + 4
    U_C0 = U_QK + 2 * PAIRS
    U_VM = U_C0 + 2
    U_C1 = U_VM + 4
    U_OM = U_C1 + 2
    U_C2 = U_OM + 4
    U_XK = U_C2 + 4
    U_WO = U_XK + KT
    U_XV = U_WO + KT
    U_XQ = U_XV + KT
    U_XO = U_XQ + KT
    U_F2 = U_XO + KT
    U_END = U_F2 + 3 * FT
    U_FFN = [0, U_F2]
    SPLIT_STEPS = [9, 10, 12, 13]
    DOWN = [(2 * FT, FT, 0), (U_WO, KT, FT), (U_XO, KT, FT + KT), (U_F2 + 2 * FT, FT, FT + 2 * KT)]
    U_CONV = [U_C0, U_C0 + 1, U_C1, U_C1 + 1, U_C2, U_C2 + 1, U_C2 + 2, U_C2 + 3]
    G_QK = NB
    G_C0 = G_QK + 2 * PAIRS
    G_VM = G_C0 + 2
    G_C1 = G_VM + NB
    G_OM = G_C1 + 2
    G_C2 = G_OM + NB
    G_CONV = [G_C0, G_C0 + 1, G_C1, G_C1 + 1, G_C2, G_C2 + 1, G_C2 + 2, G_C2 + 3]

    ctx = ExitStack()
    with ctx:
        KB = 1024
        start = -(-nc.sbuf_base // 64) * 64
        size = (nc.sbuf_usable_end - start) // 64 * 64 - 64
        ctx.enter_context(nc.sbuf_tensor("slab", [P, (size + start - nc.sbuf_base) // 4], F32))
        cursor = [start]

        def at(name, shape, offset, dt=F32):
            return nc.alloc_sbuf_tensor_at(name, shape, dt, offset=offset)

        def sb(name, shape, dt=F32):
            n = 4
            for s in shape[1:]:
                n *= s
            t = at(name, shape, cursor[0], dt)
            cursor[0] += -(-n // 32) * 32
            assert cursor[0] <= start + size, "SBUF is full"
            return t

        xn = sb("xn", [P, NB, D])
        whi = [sb(f"whi{s}", [P, D], F32R) for s in range(SPL)]
        wlo = [sb(f"wlo{s}", [P, D], F32R) for s in range(SPL)]
        raw = [sb(f"raw{s}", [P, D]) for s in range(RAW)]
        ident = sb("ident", [P, P])
        mlg = sb("mlg", [P, MW])
        gbias = sb("gbias", [MH, 2])
        relb = sb("relb", [rel_bias.shape[0], AH])
        ccol = sb("ccol", [P, CK * KT + KT])
        nmax = sb("nmax", [P, NA])
        rsum = sb("rsum", [P, NA])
        rinv = sb("rinv", [P, NA])
        acol = sb("acol", [P, NB, MH])
        emin = sb("emin", [P, NB, MH])
        den = sb("den", [P, NB])
        hst = sb("hst", [P, NB, 6])
        hmv = sb("hmv", [P, MH, NB, 2])
        hrs = sb("hrs", [P, MH, NB])
        xsum = sb("xsum", [P, NB, 2])
        nmean = sb("nmean", [P, NB])
        sqsum = sb("sqsum", [P, NB])
        rstd = sb("rstd", [P, NB])
        eps_col = sb("eps_col", [P, 1])

        gb_at = cursor[0]
        gb = at("gb", [P, 2, D], gb_at)
        craw = [at(f"craw{s}", [P, S + CK - 1], gb_at + s * 2080) for s in range(2)]
        cy = [at(f"cy{s}", [P, S], gb_at + 4160 + s * 2048) for s in range(2)]
        cursor[0] += 4160 + 4096

        hs_at = cursor[0]
        hhi = [at(f"hhi{s}", [P, S], hs_at + s * 4 * KB, F32R) for s in range(SPL)]
        hlo = [at(f"hlo{s}", [P, S], hs_at + s * 4 * KB + 2 * KB, F32R) for s in range(SPL)]
        oh_sb = at("oh_sb", [onehot.shape[0], DIST], hs_at)
        lnm_sb = at("lnm_sb", [AH, DIST], hs_at + 4 * DIST)
        tb_sb = at("tb_sb", [AH, DIST], hs_at + 8 * DIST)
        wg_raw = at("wg_raw", [P, KT, GW], hs_at + 12 * KB)
        crow = at("crow", [CK * KT + KT, P], hs_at + 12 * DIST)
        va = at("va", [P, NB, AW], hs_at)
        memn = at("memn", [P, MB, D], hs_at)
        gsp = at("gsp", [P, MH, S], hs_at + 8 * KB)
        gdiag = at("gdiag", [P, MH * NB, P], hs_at + 16 * KB)
        wb = [at(f"wb{s}", [P, S], hs_at + (8 + 2 * s) * KB) for s in range(2)]
        lg = [at(f"lg{s}", [P, S], hs_at + (18 + 2 * s) * KB) for s in range(3)]
        cursor[0] += 24 * KB

        ar = cursor[0]
        XTF = [0, ar + 121 * KB // 2]
        xth = [at("xth0", [P, KT, S], ar, F32R), at("xth1", [P, KT, S], ar + 32 * KB, F32R),
               at("xth2", [P, KT, S], ar, F32R), at("xth3", [P, KT, S], XTF[1], F32R)]
        xtl = [at("xtl0", [P, KT, S], ar + 16 * KB, F32R), at("xtl1", [P, KT, S], ar + 48 * KB, F32R),
               at("xtl2", [P, KT, S], ar + 16 * KB, F32R), at("xtl3", [P, KT, S], XTF[1] + 16 * KB, F32R)]
        hb = [at("h0", [P, FT * S], ar + 32 * KB), at("h1", [P, FT * S], ar)]
        eg = [[at(f"eg0_{s}", [P, S], ar + (76 + 2 * s) * KB) for s in range(3)],
              [at(f"eg1_{s}", [P, S], ar + (44 + 2 * s) * KB) for s in range(3)]]
        mt = [None, at("mt1", [P, KT * S], ar), at("mt2", [P, KT * S], ar + 32 * KB)]
        r_ig, r_f, r_a, r_e, r_one, r_sum = (at(f"gate_row{s}", [MH, S], ar + (2 + 2 * s) * KB) for s in range(6))
        qk = [at(f"qk{s}", [P, S], ar + (16 + 2 * s) * KB) for s in range(4)]
        om = at("om", [P, NB, MW], ar + 24 * KB)
        pt = [at(f"pt{s}", [P, S], ar + (64 + 2 * s) * KB) for s in range(PTS)]
        ob = [at(f"ob{s}", [P, NB, P], ar + (74 + 2 * s if s < 2 else 52 + 2 * s) * KB) for s in range(MH)]
        ew = [at(f"ew{s}", [P, S], ar + (78 + 2 * s) * KB) for s in range(2)]
        vx = at("vx", [P, NB, MH, P + 1], ar + 82 * KB)
        grow = at("grow", [MH, S], ar + 82 * KB + NB * MH * (P + 1) * 4)
        wg_hi = at("wg_hi", [P, KT, GW], ar + 82 * KB + NB * MH * (P + 1) * 4, F32R)
        wg_lo = at("wg_lo", [P, KT, GW], ar + 82 * KB + NB * MH * (P + 1) * 4 + KT * GW * 4, F32R)
        mth = at("mth", [P, KT, MB * P], ar + 32 * KB, F32R)
        mtl = at("mtl", [P, KT, MB * P], ar + 40 * KB, F32R)
        km = at("km", [P, KT, MB * P], ar + 48 * KB)
        xpt = [at(f"xpt{s}", [P, MB, S], ar + (56 + 4 * s) * KB) for s in range(2)]
        xp = [at(f"xp{s}", [P, MB * P], ar + (64 + s) * KB) for s in range(3)]
        vmem = at("vmem", [P, MB, D], ar + 72 * KB)
        qx = [at(f"qx{s}", [P, S], ar + (80 + 2 * s) * KB) for s in range(4)]
        squares = [at(f"squares{n}", [P, D], ar + (64 if n < 2 else 32) * KB) for n in range(4)]
        centered = [at(f"centered{n}", [P, D], ar + (68 if n < 2 else 36) * KB) for n in range(4)]
        cursor[0] += 185 * KB // 2
        assert cursor[0] <= start + size, (cursor[0], start + size)

        ps = [ctx.enter_context(nc.psum_tensor(f"ps{b}", [P, 512], F32)) for b in range(8)]

        def sem(name):
            return ctx.enter_context(nc.semaphore(name))

        x_in = [sem(f"x_in{b}") for b in range(NB)]
        raw_in = [sem(f"raw_in{s}") for s in range(RAW)]
        wb_in = [sem(f"wb_in{s}") for s in range(2)]
        small_in = sem("small_in")
        mem_in = sem("mem_in")
        gb_in = sem("gb_in")
        scr_out = sem("scr_out")
        row_out = sem("row_out")
        pool_ok = sem("pool_ok")
        pool_step = sem("pool_step")
        hi_done = sem("hi_done")
        lo_done = sem("lo_done")
        unit_used = sem("unit_used")
        hhi_done = sem("hhi_done")
        hlo_done = sem("hlo_done")
        wg_hi_done = sem("wg_hi_done")
        wg_done = sem("wg_done")
        eg_ready = sem("eg_ready")
        h_done = sem("h_done")
        grp_done = sem("grp_done")
        acc_done = sem("acc_done")
        mean_done = sem("mean_done")
        rstd_done = sem("rstd_done")
        ln_done = sem("ln_done")
        out_ready = sem("out_ready")
        xtr_done = sem("xtr_done")
        xhi_done = sem("xhi_done")
        xlo_done = sem("xlo_done")
        brow_ready = sem("brow_ready")
        brow_done = sem("brow_done")
        pj_ev = sem("pj_ev")
        grow_ready = sem("grow_ready")
        f_ready = sem("f_ready")
        ig_done = sem("ig_done")
        fabs_done = sem("fabs_done")
        flog_done = sem("flog_done")
        rows_done = sem("rows_done")
        g_out = sem("g_out")
        gsp_in = sem("gsp_in")
        gcol_ready = sem("gcol_ready")
        acol_done = sem("acol_done")
        emin_done = sem("emin_done")
        lg_ready = sem("lg_ready")
        lg_done = sem("lg_done")
        nmax_done = sem("nmax_done")
        p_done = sem("p_done")
        tr_done = sem("tr_done")
        pt_done = sem("pt_done")
        pv_done = sem("pv_done")
        o_done = sem("o_done")
        ot_done = sem("ot_done")
        mt_ev = sem("mt_ev")
        conv_y = sem("conv_y")
        conv_tanh_done = sem("conv_tanh_done")
        conv_out = sem("conv_out")
        om_done = sem("om_done")
        gdiag_done = sem("gdiag_done")
        e_done = sem("e_done")
        kq_done = sem("kq_done")
        st_done = sem("st_done")
        mpv_done = sem("mpv_done")
        fin1_done = sem("fin1_done")
        hvar_done = sem("hvar_done")
        hr_done = sem("hr_done")
        hn_done = sem("hn_done")
        mtr_done = sem("mtr_done")
        mhi_done = sem("mhi_done")
        mlo_done = sem("mlo_done")
        xv_ev = sem("xv_ev")
        xk_ev = sem("xk_ev")
        xq_ev = sem("xq_ev")
        xl_ready = sem("xl_ready")
        xm_done = sem("xm_done")
        xe_done = sem("xe_done")
        xp_done = sem("xp_done")
        xt_done = sem("xt_done")
        xt_ev = sem("xt_ev")
        xo_ready = sem("xo_ready")
        a_step = sem("a_step")
        v_step = sem("v_step")

        block = ctx.enter_context(nc.Block())

        @block.sync
        def _(sp):
            def cols(w, c0, i=None, per=0):
                v = w.rearrange("(k p) c -> p k c", p=P)
                return v[:, :, c0:c0 + P] if i is None else v[:, :, bass.ds(c0 + i * per, P)]

            def load(c, src, i=None, rearr=True):
                if i is not None or c >= RAW:
                    sp.wait_ge(lo_done, lin(c - RAW + 1, SPL, i))
                dst = raw[c % RAW][:, :]
                if len(src.shape) == 3:
                    dst = dst.rearrange("p (k c) -> p k c", k=src.shape[1])
                sp.dma_start(dst, src).then_inc(raw_in[c % RAW], 16)

            def ffn(n):
                u0 = U_FFN[n]

                def up_tile(j, i=None):
                    load(u0 + 2 * j, cols(w_gate[0, n], j * P, i, 3 * P), i)
                    load(u0 + 2 * j + 1, cols(w_up[0, n], j * P, i, 3 * P), i)

                for j in range(0 if u0 else 2, 3):
                    up_tile(j)
                with sp.Fori(1, FT // 3) as i:
                    for j in range(3):
                        up_tile(j, i)
                up_tile(FT - 1)
                d0 = u0 + 2 * FT
                with sp.Fori(0, (FT - TAIL) // SPL) as i:
                    for j in range(SPL):
                        load(d0 + j, w_down[0, n, bass.ds(j * P + i * (SPL * P), P), :], i)
                for k in range(FT - TAIL, FT):
                    load(d0 + k, w_down[0, n, k * P:(k + 1) * P, :])

            def load_x(b):
                sp.dma_start(xn[:, b, :], x[0, b * P:(b + 1) * P, :]).then_inc(x_in[b], 16)

            load_x(0)
            load_x(1)
            load(0, cols(w_gate[0, 0], 0))
            load(1, cols(w_up[0, 0], 0))
            load(2, cols(w_gate[0, 0], P))
            load_x(2)
            load(3, cols(w_up[0, 0], P))
            load_x(3)
            ffn(0)

            def rows4(u, c0):
                v = w_in[0, :, c0:c0 + 512].rearrange("(k p) c -> p k c", p=P)
                for t in range(4):
                    load(u + t, v[:, 2 * t:2 * t + 2, :])

            def conv_pair(h):
                load(U_CONV[2 * h], cols(w_in[0], 3 * AW + h * P))
                load(U_CONV[2 * h + 1], cols(w_in[0], 3 * AW + MW + h * P))

            rows4(U_VA, 2 * AW)
            for p in range(PAIRS):
                load(U_QK + 2 * p, cols(w_in[0], p * P))
                load(U_QK + 2 * p + 1, cols(w_in[0], AW + p * P))
            conv_pair(0)
            rows4(U_VM, 3 * AW + 2 * MW)
            conv_pair(1)
            rows4(U_OM, 3 * AW + 3 * MW)
            conv_pair(2)
            conv_pair(3)
            for t in range(KT):
                load(U_XK + t, cols(xkv_w[0], t * P))
            for k in range(KT):
                load(U_WO + k, w_out[0, k * P:(k + 1) * P, :])
            for k in range(KT):
                load(U_XV + k, xkv_w[0, k * P:(k + 1) * P, D:2 * D])
            for t in range(KT):
                load(U_XQ + t, cols(xq_w[0], t * P))
            for k in range(KT):
                load(U_XO + k, xo_w[0, k * P:(k + 1) * P, :])
            ffn(1)
            for b in range(NB):
                for h in range(2):
                    c = slice(h * 512, h * 512 + 512)
                    sp.wait_ge(out_ready, 2 * b + h + 1)
                    sp.dma_start(out[0, b * P:(b + 1) * P, c], xn[:, b, c]).then_inc(row_out, 16)
            sp.wait_ge(row_out, 16 * 2 * NB)

        @block.gpsimd
        def _(pool):
            nc.gpsimd.memset(ident[:, :], 0.0).then_inc(pool_step, 1)
            nc.gpsimd.memset(wg_raw[:, :, :], 0.0).then_inc(pool_step, 1)
            pool.wait_ge(pool_step, 1)
            nc.gpsimd.affine_select(out=ident[:, :], in_=ident[:, :], compare_op=ALU.not_equal, fill=1.0,
                                    base=0, pattern=[[-1, P]], channel_multiplier=1).then_inc(pool_ok, 1)
            pool.dma_start(crow[0:CK * KT, :], conv_w[0].rearrange("j (c p) -> (j c) p", p=P)).then_inc(small_in, 16)
            pool.dma_start(crow[CK * KT:, :], conv_b[0].rearrange("(c p) -> c p", p=P)).then_inc(small_in, 16)
            pool.dma_start(oh_sb[:, :], onehot).then_inc(small_in, 16)
            pool.dma_start(relb[:, :], rel_bias).then_inc(small_in, 16)
            pool.dma_start(lnm_sb[:, :], lnm).then_inc(small_in, 16)
            pool.dma_start(gbias[:, 0:1], ig_bias.rearrange("a h -> h a")).then_inc(small_in, 16)
            pool.dma_start(gbias[:, 1:2], fg_bias.rearrange("a h -> h a")).then_inc(small_in, 16)
            pool.dma_start(mlg[:, :], ml_g[0].partition_broadcast(P)).then_inc(small_in, 16)
            pool.wait_ge(pool_step, 2)
            for g in range(2):
                c = 3 * AW + 4 * MW + g * MH
                pool.dma_start(wg_raw[:, :, 32 * g:32 * g + MH],
                               w_in[0, :, c:c + MH].rearrange("(k p) c -> p k c", p=P)).then_inc(small_in, 16)
            nc.gpsimd.memset(vx[:, :, :, :], 1.0).then_inc(pool_ok, 1)

            def load_gb(n):
                pool.dma_start(gb[:, 0, :], ln_g[0, n].partition_broadcast(P)).then_inc(gb_in, 16)
                pool.dma_start(gb[:, 1, :], ln_b[0, n].partition_broadcast(P)).then_inc(gb_in, 16)

            load_gb(0)
            pool.wait_ge(brow_done, 1)
            pool.dma_start(bias_rows, tb_sb[:, :].unsqueeze(1).to_broadcast([AH, P, DIST])).then_inc(scr_out, 16)
            pool.wait_ge(scr_out, 16)
            pool.wait_ge(unit_used, U_VA)
            for h in range(AH):
                if h >= 2:
                    pool.wait_ge(lg_done, NB * (h - 1))
                src = bass.AP(bias_rows.tensor, h * P * DIST + P - 1, [[DIST - 1, P], [1, S]])
                pool.dma_start(wb[h % 2][:, :], src).then_inc(wb_in[h % 2], 16)
                if h == 1:
                    pool.wait_ge(rows_done, 1)
                    pool.dma_start(g_rows, grow[:, :]).then_inc(g_out, 16)
            pool.wait_ge(g_out, 16)
            pool.wait_ge(lg_done, NA)
            pool.dma_start(gsp[:, :, :], g_rows.partition_broadcast(P)).then_inc(gsp_in, 16)
            pool.wait_ge(gsp_in, 16)
            pool.wait_ge(tr_done, NA)
            nc.gpsimd.affine_select(out=gdiag[:, :, :], in_=gsp[:, :, :].rearrange("p h (b c) -> p (h b) c", b=NB),
                                    compare_op=ALU.is_ge, fill=1e30, base=0, pattern=[[0, MH * NB], [1, P]],
                                    channel_multiplier=-1).then_inc(gdiag_done, 1)
            pool.wait_ge(pv_done, NA)
            pool.dma_start(memn[:, :, :], mem[0].rearrange("(b p) d -> p b d", p=P)).then_inc(mem_in, 16)
            pool.wait_ge(conv_out, 2 * MH)
            load_gb(1)
            for n in (2, 3):
                pool.wait_ge(ln_done, NB * n)
                load_gb(n)

        @block.tensor
        def _(pe):
            mm = nc.tensor.matmul

            def need(u, i=None):
                pe.wait_ge(lo_done, lin(u + 1, SPL, i))

            def three(dst, lh, ll, rh, rl, start, stop):
                mm(dst, lh, rh, start=start, stop=False)
                mm(dst, lh, rl, start=False, stop=False)
                return mm(dst, ll, rh, start=False, stop=stop)

            def cols_part(u, dst, xh, xl, k0, k1, rows=slice(None), used=True):
                s = u % SPL
                for k in range(k0, k1):
                    last = three(dst, whi[s][:, k * P:(k + 1) * P], wlo[s][:, k * P:(k + 1) * P],
                                 xh[:, k, rows], xl[:, k, rows], k == 0, k == KT - 1)
                if k1 == KT and used:
                    last.then_inc(unit_used, 1)

            def transpose_rows(n, b):
                if n == 0:
                    pe.wait_ge(x_in[b], 16)
                else:
                    pe.wait_ge(ln_done, NB * (n - 1) + b + 1)
                for k in range(KT):
                    last = nc.tensor.transpose(ps[2 * b + k // 4][:, (k % 4) * P:(k % 4 + 1) * P],
                                               xn[:, b, k * P:(k + 1) * P], ident[:, :])
                last.then_inc(xtr_done, 1)

            def ffn_up(n):
                u0, xh, xl = U_FFN[n], xth[3 * n], xtl[3 * n]

                def tile(f, i=None):
                    bank = 2 * (f % 3)
                    if i is not None or n or f >= 3:
                        pe.wait_ge(h_done, lin(FT * n + f - 2, 3, i))
                    need(u0 + 2 * f, i)
                    cols_part(u0 + 2 * f, ps[bank][:, :], xh, xl, 0, KT)
                    need(u0 + 2 * f + 1, i)
                    cols_part(u0 + 2 * f + 1, ps[bank + 1][:, :], xh, xl, 0, KT)

                for half in range(2):
                    pe.wait_ge(xlo_done, NB * 3 * n + 2 * half + 2)
                    rows = slice(half * 256, half * 256 + 256)
                    for u in range(4):
                        if half == 0:
                            need(u0 + u)
                        cols_part(u0 + u, ps[u][:, rows], xh, xl, 0, KT, rows, half == 1)
                        if half == 0 and u in (1, 2):
                            transpose_rows(3 * n, u + 1)
                tile(2)
                if n == 0:
                    bias_rows_and_conv_columns()
                with pe.Fori(1, FT // 3) as i:
                    for f in range(3):
                        tile(f, i)
                tile(FT - 1)

            def product(n, k, b, start, stop, halves=(0, 1)):
                u0, nk, h0 = DOWN[n]
                u, s = u0 + k, (h0 + k) % SPL
                for half in halves:
                    c = slice(half * 512, half * 512 + 512)
                    last = three(ps[2 * b + half][:, :], hhi[s][:, b * P:(b + 1) * P],
                                 hlo[s][:, b * P:(b + 1) * P], whi[u % SPL][:, c], wlo[u % SPL][:, c],
                                 start, stop)
                return last

            def need_both(n, k, i=None):
                need(DOWN[n][0] + k, i)
                pe.wait_ge(hlo_done, lin(DOWN[n][2] + k + 1, SPL, i))

            def open_block(n, b, k0=0, k1=TAIL, used=False):
                for k in range(k0, k1):
                    if b == 3:
                        need_both(n, k)
                    last = product(n, k, b, k == 0, False)
                    if used:
                        last.then_inc(unit_used, 1)

            def down(n, order, first):
                nk = DOWN[n][1]

                def k_tile(k, i=None):
                    need_both(n, k, i)
                    opening = k == 0 and i is None
                    for b in order:
                        if opening:
                            first(b)
                        last = product(n, k, b, opening, False)
                    last.then_inc(unit_used, 1)

                if nk > KT:
                    for k in range(SPL):
                        k_tile(k)
                    with pe.Fori(1, (nk - TAIL) // SPL) as i:
                        for k in range(SPL):
                            k_tile(k, i)
                else:
                    for b in order:
                        first(b)
                        open_block(n, b, used=b == order[-1])
                for b in range(NB):
                    for half in range(2):
                        end = b == NB - 1 and half == 1
                        for k in range(nk - TAIL, nk):
                            if b == 0 and half == 0:
                                need_both(n, k)
                            last = product(n, k, b, False, k == nk - 1, (half,))
                            if end:
                                last.then_inc(unit_used, 1)
                        if not end:
                            last.then_inc(acc_done, 1)
                    if n < 3 and b in (1, 2):
                        transpose_rows(n + 1, b - 1)

            def rows_block(u0, b, dst, xh, xl):
                for t in range(4):
                    if b == 0:
                        need(u0 + t)
                    s = (u0 + t) % SPL
                    for kk in range(2):
                        k = 2 * t + kk
                        last = three(dst, xh[:, k, b * P:(b + 1) * P], xl[:, k, b * P:(b + 1) * P],
                                     whi[s][:, kk * 512:(kk + 1) * 512], wlo[s][:, kk * 512:(kk + 1) * 512],
                                     k == 0, k == KT - 1)
                    if b == NB - 1:
                        last.then_inc(unit_used, 1)
                if b < NB - 1:
                    last.then_inc(grp_done, 1)

            def bias_rows_and_conv_columns():
                pe.wait_ge(small_in, 16 * 10)
                mm(ps[6][0:AH, :], relb[:, :], oh_sb[:, 0:512], start=True, stop=True)
                mm(ps[7][0:AH, 0:DIST - 512], relb[:, :], oh_sb[:, 512:DIST], start=True, stop=True)
                nc.tensor.transpose(ps[7][:, 256:256 + CK * KT + KT], crow[:, :],
                                    ident[0:CK * KT + KT, 0:CK * KT + KT]).then_inc(brow_ready, 1)

            def warm(count):
                for _ in range(count):
                    mm(ps[7][:, 0:P], ident[:, :], ident[:, :], start=True, stop=True)

            pe.wait_ge(pool_ok, 1)
            warm(6)
            transpose_rows(0, 0)
            transpose_rows(0, 1)
            warm(8)
            ffn_up(0)
            down(0, (3, 1, 2, 0), lambda b: pe.wait_ge(*{3: (brow_done, 1), 1: (h_done, FT - 2), 2: (h_done, FT - 1),
                                                         0: (h_done, FT)}[b]))

            xh, xl = xth[1], xtl[1]
            for b in range(NB):
                if b in (1, 2):
                    transpose_rows(1, b + 1)
                pe.wait_ge(xlo_done, NB + b + 1)
                rows_block(U_VA, b, ps[2 * b][:, :], xh, xl)
            pe.wait_ge(wg_done, 1)
            for k in range(KT):
                last = three(ps[1][0:GW, :], wg_hi[:, k, :], wg_lo[:, k, :], xh[:, k, :], xl[:, k, :], k == 0, k == KT - 1)
            last.then_inc(grow_ready, 1)

            def project(u, g, k0=0, k1=KT):
                if k0 == 0:
                    need(u)
                    pe.wait_ge(pj_ev, g if g == G_QK else g - 1)
                cols_part(u, ps[6 + g % 2][:, :], xh, xl, k0, k1)

            project(U_QK, G_QK)
            project(U_QK + 1, G_QK + 1)
            def gate_columns():
                pe.wait_ge(rows_done, 1)
                for c in range(NB):
                    nc.tensor.transpose(ps[5][:, c * MH:(c + 1) * MH], r_a[:, c * P:(c + 1) * P], ident[0:MH, 0:MH])
                    last = nc.tensor.transpose(ps[5][:, 16 + c * MH:16 + (c + 1) * MH], r_f[:, c * P:(c + 1) * P],
                                               ident[0:MH, 0:MH])
                last.then_inc(gcol_ready, 1)

            def logits(n):
                h, i = divmod(n, NB)
                p = h // 2
                if n % (2 * NB) == 0:
                    pe.wait_ge(pj_ev, G_QK + 2 * p + 2)
                if n == 1:
                    pe.wait_ge(ig_done, 1)
                if n >= 2:
                    pe.wait_ge(lg_done, n - 1)
                rows = slice((h % 2) * HD, (h % 2) * HD + HD)
                mm(ps[n % 2][:, 0:(i + 1) * P], qk[(2 * p) % 4][rows, i * P:(i + 1) * P],
                   qk[(2 * p + 1) % 4][rows, 0:(i + 1) * P], start=True, stop=True).then_inc(lg_ready, 1)

            def transpose_p(n):
                pe.wait_ge(p_done, n + 1)
                if n >= 2:
                    pe.wait_ge(pt_done, n - 1)
                if n >= 11 and n % 8 == 3:
                    pe.wait_ge(mt_ev, (n - 11) // 8 + 1)
                for j in range(n % NB + 1):
                    last = nc.tensor.transpose(ps[2 + n % 2][:, j * P:(j + 1) * P],
                                               lg[n % 3][:, j * P:(j + 1) * P], ident[:, :])
                last.then_inc(tr_done, 1)

            def values(n):
                h, i = divmod(n, NB)
                pe.wait_ge(pt_done, n + 1)
                if n == 1:
                    pe.wait_ge(acol_done, 1)
                    pe.wait_ge(emin_done, 1)
                if n >= 2:
                    pe.wait_ge(o_done, n - 1)
                for j in range(i + 1):
                    last = mm(ps[4 + n % 2][:, 0:HD], pt[n % PTS][:, j * P:(j + 1) * P],
                              va[:, j, h * HD:(h + 1) * HD], start=j == 0, stop=j == i)
                last.then_inc(pv_done, 1)

            def transpose_o(t):
                if t < PAIRS:
                    pe.wait_ge(o_done, 2 * NB * (t + 1))
                    pe.wait_ge(pt_done, min(8 * t + 10, NA))
                else:
                    pe.wait_ge(hn_done, t - PAIRS + 1)
                if t:
                    pe.wait_ge(mt_ev, t)
                o = ob[t % 2 if t < PAIRS else t - PAIRS]
                for i in range(NB):
                    last = nc.tensor.transpose(ps[3][:, i * P:(i + 1) * P], o[:, i, :], ident[:, :])
                last.then_inc(ot_done, 1)

            def attention(n):
                if 2 <= n < NA + 2:
                    transpose_p(n - 2)
                if n < NA and n % 8:
                    logits(n)
                if 3 <= n < NA + 3:
                    values(n - 3)
                if n < NA and n % 8 == 0:
                    logits(n)

            for n in range(NA):
                q = 2 + n // 4
                quarter = (U_QK + q, G_QK + q, 2 * (n % 4), 2 * (n % 4) + 2)
                if n % 8 == 0:
                    project(*quarter)
                attention(n)
                if n % 8 == 4 and n >= 12:
                    transpose_o((n - 12) // 8)
                if n == 2:
                    gate_columns()
                if n % 8:
                    project(*quarter)

            def rows_group(u0, g, b):
                pe.wait_ge(pj_ev, g + b - 1)
                rows_block(u0, b, ps[6 + (g + b) % 2][:, :], xh, xl)

            for b in range(3):
                attention(NA + b)
                rows_group(U_VM, G_VM, b)
            transpose_o(PAIRS - 1)
            rows_group(U_VM, G_VM, 3)

            def kq(h, j):
                s = NB * h + j
                if j == 0:
                    pe.wait_ge(conv_out, 2 * h + 2)
                if s < 2:
                    pe.wait_ge(lg_done, NA)
                else:
                    pe.wait_ge(st_done, s - 1)
                mm(ps[j % 2][:, 0:S - j * P], qk[(2 * h + 1) % 4][:, j * P:(j + 1) * P],
                   qk[(2 * h) % 4][:, j * P:S], start=True, stop=True).then_inc(kq_done, 1)

            def numerators(h):
                pe.wait_ge(st_done, NB * (h + 1))
                if h == 0:
                    pe.wait_ge(pj_ev, G_VM + NB)
                    pe.wait_ge(pool_ok, 2)
                    pe.wait_ge(o_done, NA)
                else:
                    pe.wait_ge(fin1_done, h)
                for i in range(NB):
                    c = 256 * (i % 2)
                    for j in range(i + 1):
                        slot = (NA + NB * h + j) % PTS
                        last = mm(ps[4 + i // 2][:, c:c + P + 1], pt[slot][:, (i - j) * P:(i - j + 1) * P],
                                  vx[:, j, h, :], start=j == 0, stop=j == i)
                last.then_inc(mpv_done, 1)

            def transpose_mem(b):
                if b == 0:
                    pe.wait_ge(mem_in, 16)
                    pe.wait_ge(pj_ev, G_C2 + 4)
                else:
                    pe.wait_ge(mlo_done, b)
                for k in range(KT):
                    last = nc.tensor.transpose(ps[6 + k // 4][:, (k % 4) * P:(k % 4 + 1) * P],
                                               memn[:, b, k * P:(k + 1) * P], ident[:, :])
                last.then_inc(mtr_done, 1)

            def mem_key(t):
                if t == 0:
                    pe.wait_ge(mlo_done, MB)
                elif t >= 2:
                    pe.wait_ge(xk_ev, t - 1)
                need(U_XK + t)
                cols_part(U_XK + t, ps[6 + t % 2][:, 0:MB * P], mth, mtl, 0, KT)

            for h in range(MH):
                kq(h, 0)
                kq(h, 1)
                if h == 0:
                    project(U_C1, G_C1)
                elif h == 1:
                    project(U_C2, G_C2)
                elif h == 2:
                    transpose_mem(0)
                else:
                    mem_key(2)
                kq(h, 2)
                kq(h, 3)
                if h == 0:
                    project(U_C1 + 1, G_C1 + 1)
                    rows_group(U_OM, G_OM, 0)
                elif h == 1:
                    project(U_C2 + 1, G_C2 + 1)
                elif h == 2:
                    transpose_mem(1)
                else:
                    mem_key(3)
                numerators(h)
                if h == 0:
                    for b in range(1, NB):
                        rows_group(U_OM, G_OM, b)
                elif h == 1:
                    project(U_C2 + 2, G_C2 + 2)
                    project(U_C2 + 3, G_C2 + 3)
                elif h == 2:
                    mem_key(0)
                    mem_key(1)
            mem_key(4)
            for h in range(MH - 1):
                mem_key(5 + h)
                transpose_o(PAIRS + h)

            def first(b):
                if b == 3:
                    pe.wait_ge(xk_ev, KT)
                elif b == 0:
                    pe.wait_ge(st_done, NB * MH)
                elif b == 2:
                    transpose_o(KT - 1)
                    pe.wait_ge(fin1_done, MH)
                else:
                    pe.wait_ge(mt_ev, KT)
            down(1, (3, 0, 2, 1), first)

            pe.wait_ge(xlo_done, NB * 2 + 2)
            for k in range(KT):
                if k in (2, 4):
                    transpose_rows(2, 1 + k // 2)
                u = U_XV + k
                need(u)
                for b in range(MB):
                    for half in range(2):
                        c = slice(half * 512, half * 512 + 512)
                        last = three(ps[2 * b + half][:, :], mth[:, k, b * P:(b + 1) * P],
                                     mtl[:, k, b * P:(b + 1) * P], whi[u % SPL][:, c], wlo[u % SPL][:, c],
                                     k == 0, k == KT - 1)
                last.then_inc(unit_used, 1)

            def query(t, k0=0, k1=KT):
                if k0 == 0:
                    if t >= 2:
                        pe.wait_ge(xq_ev, t - 1)
                    need(U_XQ + t)
                cols_part(U_XQ + t, ps[6 + t % 2][:, :], xth[2], xtl[2], k0, k1)

            pe.wait_ge(xlo_done, NB * 3)
            query(0)
            query(1)
            for n in range(NX + 4):
                if 2 <= n < NX + 2:
                    m = n - 2
                    pe.wait_ge(xp_done, m + 1)
                    if m >= 2:
                        pe.wait_ge(xt_ev, m - 1)
                    for b in range(MB):
                        last = nc.tensor.transpose(ps[2 + m % 2][:, b * P:(b + 1) * P],
                                                   xp[m % 3][:, b * P:(b + 1) * P], ident[:, :])
                    last.then_inc(xt_done, 1)
                if n < NX - NB and n % NB == 0:
                    query(2 + n // 2, 0, 4)
                elif n == NX - NB:
                    need_both(2, 0)
                    pe.wait_ge(xq_ev, KT - 1)
                    product(2, 0, 3, True, False, (0,))
                if n < NX:
                    h, i = divmod(n, NB)
                    if i == 0:
                        pe.wait_ge(xq_ev, 2 * h + 2)
                    if n == 0:
                        pe.wait_ge(xv_ev, 2 * MB)
                    if n >= 2:
                        pe.wait_ge(xe_done, n - 1)
                    for c in range(2):
                        last = mm(ps[n % 2][:, 0:MB * P], qx[(2 * h + c) % 4][:, i * P:(i + 1) * P],
                                  km[:, 2 * h + c, :], start=c == 0, stop=c == 1)
                    last.then_inc(xl_ready, 1)
                if n >= 6 and (n - 6) % NB < 2:
                    h, c = divmod(n - 6, NB)
                    if c == 0:
                        pe.wait_ge(xt_ev, NB * (h + 1))
                    if h:
                        pe.wait_ge(mt_ev, KT + 2 * h - 1 + c)
                    for b in range(MB):
                        last = mm(ps[4 + c][:, :], vmem[:, b, (2 * h + c) * P:(2 * h + c + 1) * P],
                                  xpt[h % 2][:, b, :], start=b == 0, stop=b == MB - 1)
                    last.then_inc(xo_ready, 1)
                if n < NX - NB:
                    if n % NB:
                        query(2 + n // 2, 4 * (n % 2), 4 * (n % 2) + 4)
                elif n < NX:
                    if n == NX - NB:
                        product(2, 0, 3, True, False, (1,))
                    else:
                        open_block(2, 3, n - NX + NB, n - NX + NB + 1)
                elif n == NX:
                    pe.wait_ge(xe_done, NX)
                    open_block(2, 0, 0, 2)
                elif n == NX + 1:
                    open_block(2, 0, 2, 4)

            down(2, (1, 2), lambda b: pe.wait_ge(*{1: (xt_ev, NX), 2: (mt_ev, 2 * KT)}[b]))

            ffn_up(1)
            down(3, (3, 1, 2, 0), lambda b: pe.wait_ge(h_done, {3: 1, 1: 2 * FT - 2, 2: 2 * FT - 1, 0: 2 * FT}[b]))

        @block.scalar
        def _(act):
            step = Steps(act, a_step)

            def fn(*a, **k):
                return nc.scalar.activation(*a, **k)

            def split(c, i=None):
                if c >= U_END:
                    return
                act.wait_ge(raw_in[c % RAW], lin(16 * (c // RAW + 1), 16 * SPL // RAW, i))
                if i is not None or c >= SPL:
                    act.wait_ge(unit_used, lin(c - SPL + 1, SPL, i))
                fn(whi[c % SPL][:, :], raw[c % RAW][:, :], ACT.Copy).then_inc(hi_done, 1)

            def split_act(n, k, src, i=None):
                u0, nk, h0 = DOWN[n]
                if i is not None or k >= SPL:
                    act.wait_ge(unit_used, lin(u0 + k - SPL + 1, SPL, i))
                fn(hhi[(h0 + k) % SPL][:, :], src, ACT.Copy).then_inc(hhi_done, 1)

            def x_hi(n, b):
                act.wait_ge(xtr_done, NB * n + b + 1)
                for h in range(2):
                    fn(xth[n][:, 4 * h:4 * h + 4, b * P:(b + 1) * P],
                       ps[2 * b + h][:, :].rearrange("p (k c) -> p k c", k=4), ACT.Copy).then_inc(xhi_done, 1)

            def inv_std(n, b):
                act.wait_ge(mean_done, NB * n + b + 1)
                step.link(fn(squares[n][:, :], xn[:, b, :], ACT.Square, bias=nmean[:, b:b + 1],
                             accum_out=sqsum[:, b:b + 1]))
                step.link(fn(rstd[:, b:b + 1], sqsum[:, b:b + 1], ACT.Ln, scale=1.0 / D, bias=eps_col[:, 0:1]))
                fn(rstd[:, b:b + 1], rstd[:, b:b + 1], ACT.Exp, scale=-0.5).then_inc(rstd_done, 1)

            def h_tile(n, k, i=None):
                if i is None:
                    return hb[n][:, k * S:(k + 1) * S]
                return hb[n][:, bass.ds(k * S + i * (SPL * S), S)]

            def split_h(n, k, i=None):
                act.wait_ge(h_done, lin(FT * n + k + 1, SPL, i))
                split_act(3 * n, k, h_tile(n, k, i), i)

            def split_mt(n, k):
                act.wait_ge(mt_ev, KT * (n - 1) + k + 1)
                split_act(n, k, mt[n][:, k * S:(k + 1) * S])

            def ffn_up(n):
                u0 = U_FFN[n]
                act.preload_act_table_set("exp_and_others")

                def tile(f, i=None):
                    split(u0 + 2 * f + AHEAD, i)
                    act.wait_ge(unit_used, lin(u0 + 2 * f + 1, SPL, i))
                    if i is not None or n or f >= 3:
                        act.wait_ge(h_done, lin(FT * n + f - 2, 3, i))
                    fn(eg[n][f % 3][:, :], ps[2 * (f % 3)][:, :], ACT.Tanh, scale=0.5).then_inc(eg_ready, 1)
                    split(u0 + 2 * f + AHEAD + 1, i)

                for f in range(3):
                    tile(f)
                if n == 0:
                    act.wait_ge(small_in, 16 * 10)
                    fn(wg_hi[:, :, :], wg_raw[:, :, :], ACT.Copy).then_inc(wg_hi_done, 1)
                with act.Fori(1, FT // 3) as i:
                    for f in range(3):
                        tile(f, i)
                if n == 0:
                    act.wait_ge(scr_out, 16)
                for k in range(3):
                    split_h(n, k)
                tile(FT - 1)

            def ffn_down(n):
                u0 = DOWN[3 * n][0]
                act.preload_act_table_set("natural_log_exp_and_others")
                with act.Fori(0, (FT - TAIL) // SPL) as i:
                    for k in range(SPL):
                        split(u0 + k + AHEAD, i)
                        split_h(n, k + 3, i)
                split_h(n, FT - 1)
                tail(3 * n)

            def mt_down(n):
                split(DOWN[n][0] + AHEAD)
                split(DOWN[n][0] + 1 + AHEAD)
                for k in range(4, KT):
                    split_mt(n, k)
                    if k < 6:
                        split(DOWN[n][0] + k - 2 + AHEAD)
                tail(n)

            def tail(n):
                ut = DOWN[n][0] + DOWN[n][1] - TAIL
                split(ut + AHEAD)
                inv_std(n, 0)
                split(ut + AHEAD + 1)
                inv_std(n, 1)
                if n < 3:
                    x_hi(n + 1, 0)
                inv_std(n, 2)
                if n < 3:
                    x_hi(n + 1, 1)
                split(ut + AHEAD + 2)
                split(ut + AHEAD + 3)
                inv_std(n, 3)
                if n < 3:
                    x_hi(n + 1, 2)

            x_hi(0, 0)
            x_hi(0, 1)
            split(0)
            split(1)
            split(2)
            split(3)
            x_hi(0, 2)
            x_hi(0, 3)
            ffn_up(0)
            ffn_down(0)

            def evacuate(g, dst, ready, value, func=ACT.Copy, scale=1.0, bank=None):
                act.wait_ge(ready, value)
                src = ps[6 + g % 2 if bank is None else bank][:, :]
                if len(dst.shape) == 3:
                    src = src.rearrange("p (h c) -> p h c", h=dst.shape[1])
                fn(dst, src, func, scale=scale).then_inc(pj_ev, 1)

            def va_block(b):
                ready = (grp_done, b + 1) if b < 3 else (unit_used, U_VA + 4)
                evacuate(b, va[:, b, :], *ready, bank=2 * b)

            split(U_VA + 4)
            va_block(0)
            split(U_VA + 5)
            va_block(1)
            x_hi(1, 3)
            va_block(2)
            split(U_VA + 6)
            split(U_VA + 7)
            va_block(3)
            act.wait_ge(grow_ready, 1)
            fn(r_f[:, :], ps[1][32:GW, :], ACT.Copy).then_inc(f_ready, 1)

            def qk_tile(t):
                evacuate(G_QK + t, qk[t % 4][:, :], unit_used, U_QK + t + 1)

            def conv_tile(t):
                if t >= 2:
                    act.wait_ge(conv_out, t - 1)
                evacuate(G_CONV[t], craw[t % 2][:, CK - 1:], unit_used, U_CONV[t] + 1)

            def conv_tanh(t):
                act.wait_ge(conv_y, t + 1)
                fn(craw[t % 2][:, CK - 1:], cy[t % 2][:, :], ACT.Tanh, scale=0.5).then_inc(conv_tanh_done, 1)

            split(U_QK + 4)
            qk_tile(0)
            act.wait_ge(fabs_done, 1)
            step.link(fn(r_e[:, :], r_e[:, :], ACT.Exp, scale=-1.0))
            fn(r_e[:, :], r_e[:, :], ACT.Ln, bias=1.0).then_inc(flog_done, 1)
            split(U_QK + 5)
            qk_tile(1)
            act.preload_act_table_set("exp_and_others")

            def exp_min():
                act.wait_ge(gcol_ready, 1)
                act.wait_ge(acol_done, 1)
                fn(emin[:, :, :], ps[5][:, 16:32].rearrange("p (b c) -> p b c", b=NB), ACT.Exp)\
                    .then_inc(emin_done, 1)

            def probs(n):
                w = (n % NB + 1) * P
                act.wait_ge(nmax_done, n + 1)
                fn(lg[n % 3][:, 0:w], lg[n % 3][:, 0:w], ACT.Exp, bias=nmax[:, n:n + 1],
                   accum_out=rsum[:, n:n + 1]).then_inc(p_done, 1)

            def p_copy(n):
                w = (n % NB + 1) * P
                act.wait_ge(tr_done, n + 1)
                if n >= PTS:
                    act.wait_ge(pv_done, n - PTS + 1)
                fn(pt[n % PTS][:, 0:w], ps[2 + n % 2][:, 0:w], ACT.Copy).then_inc(pt_done, 1)

            def mt_copy(t):
                act.wait_ge(ot_done, t + 1)
                fn(mt[1][:, t * S:(t + 1) * S], ps[3][:, :], ACT.Copy).then_inc(mt_ev, 1)

            for n in range(NA):
                if n % 4 == 0:
                    t = 1 + n // 4
                    if 2 <= t < 2 * PAIRS:
                        qk_tile(t)
                    elif t >= 2:
                        conv_tile(t - 2 * PAIRS)
                if n >= 2:
                    p_copy(n - 2)
                if n % 8 == 4 and n >= 12:
                    mt_copy((n - 12) // 8)
                probs(n)
                if n == 2:
                    exp_min()
                if n % 4 == 2:
                    split(U_QK + 2 + n // 4 + AHEAD)
            conv_tanh(0)
            conv_tile(1)
            p_copy(NA - 2)
            split(U_VM + 4)

            def vm_block(b):
                ready = (grp_done, 3 + b + 1) if b < 3 else (unit_used, U_VM + 4)
                evacuate(G_VM + b, vx[:, b, :, 0:P], *ready)

            def om_block(b):
                ready = (grp_done, 6 + b + 1) if b < 3 else (unit_used, U_OM + 4)
                evacuate(G_OM + b, om[:, b, :], *ready, func=ACT.Tanh, scale=0.5)

            act.wait_ge(pool_ok, 2)
            vm_block(0)
            p_copy(NA - 1)
            split(U_VM + 5)
            vm_block(1)
            conv_tanh(1)
            vm_block(2)
            mt_copy(PAIRS - 1)
            split(U_VM + 6)
            split(U_VM + 7)
            vm_block(3)

            def weights(h, j):
                s = NB * h + j
                if s == 0:
                    act.wait_ge(gsp_in, 16)
                    act.wait_ge(gdiag_done, 1)
                    act.wait_ge(acol_done, 1)
                if s >= 2:
                    act.wait_ge(st_done, s - 1)
                last = fn(ew[j % 2][:, 0:P], gdiag[:, s, :], ACT.Exp, scale=-1.0, bias=acol[:, j, h:h + 1])
                if j < NB - 1:
                    last = fn(ew[j % 2][:, P:S - j * P], gsp[:, h, (j + 1) * P:S], ACT.Exp, scale=-1.0,
                              bias=acol[:, j, h:h + 1])
                last.then_inc(e_done, 1)

            def head_std(h0, h1):
                act.wait_ge(hvar_done, h1)
                step.link(fn(hrs[:, h0:h1, :], hmv[:, h0:h1, :, 1], ACT.Ln, bias=eps_col[:, 0:1]))
                fn(hrs[:, h0:h1, :], hrs[:, h0:h1, :], ACT.Exp, scale=-0.5).then_inc(hr_done, 1)

            def mem_hi(b):
                act.wait_ge(mtr_done, b + 1)
                for h in range(2):
                    fn(mth[:, 4 * h:4 * h + 4, b * P:(b + 1) * P],
                       ps[6 + h][:, :].rearrange("p (k c) -> p k c", k=4), ACT.Copy).then_inc(mhi_done, 1)

            def key_tile(t):
                act.wait_ge(unit_used, U_XK + t + 1)
                fn(km[:, t, :], ps[6 + t % 2][:, 0:MB * P], ACT.Copy).then_inc(xk_ev, 1)

            weights(0, 0)
            weights(0, 1)
            split(U_C1 + AHEAD)
            conv_tile(2)
            weights(0, 2)
            weights(0, 3)
            split(U_C1 + 1 + AHEAD)
            conv_tile(3)
            conv_tanh(2)
            om_block(0)
            split(U_OM + 4)
            conv_tanh(3)
            om_block(1)
            split(U_OM + 5)
            om_block(2)
            split(U_OM + 6)
            split(U_OM + 7)
            om_block(3)
            weights(1, 0)
            weights(1, 1)
            split(U_C2 + AHEAD)
            conv_tile(4)
            weights(1, 2)
            weights(1, 3)
            split(U_C2 + 1 + AHEAD)
            conv_tanh(4)
            conv_tile(5)
            conv_tanh(5)
            split(U_C2 + 2 + AHEAD)
            conv_tile(6)
            split(U_C2 + 3 + AHEAD)
            conv_tile(7)
            conv_tanh(6)
            weights(2, 0)
            weights(2, 1)
            mem_hi(0)
            weights(2, 2)
            weights(2, 3)
            mem_hi(1)
            conv_tanh(7)
            weights(3, 0)
            weights(3, 1)
            for t in range(2):
                split(U_XK + t + AHEAD)
                key_tile(t)
            weights(3, 2)
            weights(3, 3)
            split(U_XK + 2 + AHEAD)
            key_tile(2)
            act.preload_act_table_set("natural_log_exp_and_others")
            head_std(0, MH - 1)
            for t in range(3, 5):
                split(U_XK + t + AHEAD)
                key_tile(t)
            split_mt(1, 0)
            split_mt(1, 1)
            for h in range(MH - 1):
                split(U_XK + 5 + h + AHEAD)
                key_tile(5 + h)
                mt_copy(PAIRS + h)
                if h < 2:
                    split_mt(1, 2 + h)
            head_std(MH - 1, MH)
            mt_copy(KT - 1)
            mt_down(1)

            for k in range(KT):
                split(U_XV + k + AHEAD)
                if k == 4:
                    x_hi(2, 3)
            act.wait_ge(unit_used, U_XV + KT)
            for b in range(MB):
                for h in range(2):
                    fn(vmem[:, b, h * 512:(h + 1) * 512], ps[2 * b + h][:, :], ACT.Copy).then_inc(xv_ev, 1)

            def query(t):
                act.wait_ge(unit_used, U_XQ + t + 1)
                fn(qx[t % 4][:, :], ps[6 + t % 2][:, :], ACT.Copy, scale=XSCALE).then_inc(xq_ev, 1)

            split(U_XQ + AHEAD)
            query(0)
            split(U_XQ + 1 + AHEAD)
            query(1)
            for n in range(NX + 5):
                if n % 2 == 0 and 2 <= n <= 12:
                    query(1 + n // 2)
                if 2 <= n < NX + 2:
                    h, i = divmod(n - 2, NB)
                    act.wait_ge(xt_done, n - 1)
                    if h >= 2:
                        act.wait_ge(xo_ready, 2 * (h - 1))
                    fn(xpt[h % 2][:, :, i * P:(i + 1) * P],
                       ps[2 + n % 2][:, 0:MB * P].rearrange("p (b c) -> p b c", b=MB), ACT.Copy).then_inc(xt_ev, 1)
                if n < NX:
                    act.wait_ge(xm_done, n + 1)
                    if n >= 3:
                        act.wait_ge(xt_done, n - 2)
                    fn(xp[n % 3][:, :], ps[n % 2][:, 0:MB * P], ACT.Exp, bias=nmax[:, n:n + 1],
                       accum_out=rsum[:, n:n + 1]).then_inc(xe_done, 1)
                if n % 2 == 1 and n < 12:
                    split(U_XQ + 2 + n // 2 + AHEAD)
                if n >= 7 and (n - 7) % NB < 2:
                    h, c = divmod(n - 7, NB)
                    t = 2 * h + c
                    act.wait_ge(xo_ready, t + 1)
                    fn(mt[2][:, t * S:(t + 1) * S], ps[4 + c][:, :], ACT.Copy).then_inc(mt_ev, 1)
                if n in SPLIT_STEPS:
                    split_mt(2, SPLIT_STEPS.index(n))
            mt_down(2)
            x_hi(3, 3)
            ffn_up(1)
            ffn_down(1)

        @block.vector
        def _(dve):
            v = nc.vector
            step = Steps(dve, v_step)

            def split(c, i=None):
                if c >= U_END:
                    return
                dve.wait_ge(hi_done, lin(c + 1, SPL, i))
                v.tensor_tensor(wlo[c % SPL][:, :], raw[c % RAW][:, :], whi[c % SPL][:, :].bitcast(F32),
                                ALU.subtract).then_inc(lo_done, 1)

            def split_act(n, k, src, i=None):
                u0, nk, h0 = DOWN[n]
                s = (h0 + k) % SPL
                dve.wait_ge(hhi_done, lin(h0 + k + 1, SPL, i))
                v.tensor_tensor(hlo[s][:, :], src, hhi[s][:, :].bitcast(F32), ALU.subtract).then_inc(hlo_done, 1)

            def x_lo(n, b):
                for h in range(2):
                    dve.wait_ge(xhi_done, 2 * (NB * n + b) + h + 1)
                    blk = (slice(None), slice(4 * h, 4 * h + 4), slice(b * P, (b + 1) * P))
                    last = v.tensor_tensor(xtl[n][blk], ps[2 * b + h][:, :].rearrange("p (k c) -> p k c", k=4),
                                           xth[n][blk].bitcast(F32), ALU.subtract)
                last.then_inc(xlo_done, 1)

            def norm(n, b):
                for h in range(2):
                    if b < NB - 1 or h == 0:
                        dve.wait_ge(acc_done, (2 * NB - 1) * n + 2 * b + h + 1)
                    else:
                        dve.wait_ge(unit_used, DOWN[n][0] + DOWN[n][1])
                    half = xn[:, b, h * 512:(h + 1) * 512]
                    step.inc(v.scalar_tensor_tensor(out=half, in0=half, scalar=ALPHA, in1=ps[2 * b + h][:, :],
                                                    op0=ALU.mult, op1=ALU.add, accum_out=xsum[:, b, h:h + 1]))
                dve.wait_ge(v_step, step.base + step.k)
                v.tensor_scalar(nmean[:, b:b + 1], xsum[:, b, 0:1], xsum[:, b, 1:2], -1.0 / D, ALU.add, ALU.mult)\
                    .then_inc(mean_done, 1)
                dve.wait_ge(gb_in, 32 * (n + 1))
                dve.wait_ge(mean_done, NB * n + b + 1)
                step.link(v.scalar_tensor_tensor(out=centered[n][:, :], in0=xn[:, b, :], scalar=nmean[:, b:b + 1],
                                                 in1=gb[:, 0, :], op0=ALU.add, op1=ALU.mult))
                dve.wait_ge(rstd_done, NB * n + b + 1)
                if n < 3:
                    v.scalar_tensor_tensor(out=xn[:, b, :], in0=centered[n][:, :], scalar=rstd[:, b:b + 1],
                                           in1=gb[:, 1, :], op0=ALU.mult, op1=ALU.add).then_inc(ln_done, 1)
                else:
                    for h in range(2):
                        c = slice(h * 512, h * 512 + 512)
                        v.scalar_tensor_tensor(out=xn[:, b, c], in0=centered[n][:, c], scalar=rstd[:, b:b + 1],
                                               in1=gb[:, 1, c], op0=ALU.mult, op1=ALU.add).then_inc(out_ready, 1)

            def split_h(n, k, i=None):
                src = hb[n][:, k * S:(k + 1) * S] if i is None else hb[n][:, bass.ds(k * S + i * (SPL * S), S)]
                split_act(3 * n, k, src, i)

            def split_mt(n, k):
                split_act(n, k, mt[n][:, k * S:(k + 1) * S])

            def ffn_up(n):
                u0 = U_FFN[n]

                def tile(f, i=None):
                    split(u0 + 2 * f + AHEAD, i)
                    split(u0 + 2 * f + AHEAD + 1, i)
                    e, bank = eg[n][f % 3], 2 * (f % 3)
                    dve.wait_ge(eg_ready, lin(FT * n + f + 1, 3, i))
                    step.link(v.scalar_tensor_tensor(out=e[:, :], in0=e[:, :], scalar=1.0, in1=ps[bank][:, :],
                                                     op0=ALU.add, op1=ALU.mult))
                    dve.wait_ge(unit_used, lin(u0 + 2 * f + 2, SPL, i))
                    dst = hb[n][:, f * S:(f + 1) * S] if i is None else hb[n][:, bass.ds(f * S + i * (3 * S), S)]
                    v.scalar_tensor_tensor(out=dst, in0=e[:, :], scalar=0.25, in1=ps[bank + 1][:, :],
                                           op0=ALU.mult, op1=ALU.mult).then_inc(h_done, 1)

                for f in range(3):
                    tile(f)
                if n == 0:
                    dve.wait_ge(brow_ready, 1)
                    step.inc(v.tensor_tensor(tb_sb[:, 0:512], ps[6][0:AH, :], lnm_sb[:, 0:512], ALU.add))
                    step.inc(v.tensor_tensor(tb_sb[:, 512:DIST], ps[7][0:AH, 0:DIST - 512], lnm_sb[:, 512:DIST], ALU.add))
                    dve.wait_ge(v_step, step.k)
                    v.tensor_copy(ccol[:, :], ps[7][:, 256:256 + CK * KT + KT]).then_inc(brow_done, 1)
                    dve.wait_ge(wg_hi_done, 1)
                    v.tensor_tensor(wg_lo[:, :, :], wg_raw[:, :, :], wg_hi[:, :, :].bitcast(F32), ALU.subtract)\
                        .then_inc(wg_done, 1)
                with dve.Fori(1, FT // 3) as i:
                    step.enter(i - 1, 3)
                    for f in range(3):
                        tile(f, i)
                step.leave(FT // 3 - 1, 3)
                for k in range(3):
                    split_h(n, k)
                tile(FT - 1)

            def ffn_down(n):
                u0 = DOWN[3 * n][0]
                with dve.Fori(0, (FT - TAIL) // SPL) as i:
                    for k in range(SPL):
                        split(u0 + k + AHEAD, i)
                        split_h(n, k + 3, i)
                split_h(n, FT - 1)
                tail(3 * n)

            def mt_down(n):
                split(DOWN[n][0] + AHEAD)
                split(DOWN[n][0] + 1 + AHEAD)
                for k in range(4, KT):
                    split_mt(n, k)
                    if k < 6:
                        split(DOWN[n][0] + k - 2 + AHEAD)
                tail(n)

            def tail(n):
                ut = DOWN[n][0] + DOWN[n][1] - TAIL
                split(ut + AHEAD)
                norm(n, 0)
                split(ut + AHEAD + 1)
                norm(n, 1)
                if n < 3:
                    x_lo(n + 1, 0)
                norm(n, 2)
                if n < 3:
                    x_lo(n + 1, 1)
                split(ut + AHEAD + 2)
                split(ut + AHEAD + 3)
                norm(n, 3)
                if n < 3:
                    x_lo(n + 1, 2)

            step.link(v.memset(eps_col[:, :], LN_EPS))
            x_lo(0, 0)
            x_lo(0, 1)
            split(0)
            split(1)
            split(2)
            split(3)
            x_lo(0, 2)
            x_lo(0, 3)
            ffn_up(0)
            ffn_down(0)

            split(U_VA + 4)
            split(U_VA + 5)
            x_lo(1, 3)
            split(U_VA + 6)
            split(U_VA + 7)
            for s in range(2):
                step.link(v.memset(craw[s][:, 0:CK - 1], 0.0))
            step.link(v.memset(r_one[:, :], 1.0))
            split(U_QK + 4)
            dve.wait_ge(f_ready, 1)
            step.link(v.tensor_scalar(r_f[:, :], r_f[:, :], gbias[:, 1:2], None, ALU.add))
            v.scalar_tensor_tensor(out=r_e[:, :], in0=r_f[:, :], scalar=-1.0, in1=r_f[:, :],
                                   op0=ALU.mult, op1=ALU.max).then_inc(fabs_done, 1)
            v.tensor_scalar(r_ig[:, :], ps[1][0:MH, :], gbias[:, 0:1], None, ALU.add).then_inc(ig_done, 1)
            dve.wait_ge(flog_done, 1)
            step.link(v.scalar_tensor_tensor(out=r_f[:, :], in0=r_f[:, :], scalar=0.0, in1=r_e[:, :],
                                             op0=ALU.min, op1=ALU.subtract))
            step.link(v.tensor_tensor_scan(r_sum[:, :], r_one[:, :], r_f[:, :], 0.0, ALU.mult, ALU.add))
            dve.wait_ge(ig_done, 1)
            step.link(v.tensor_tensor(r_a[:, :], r_ig[:, :], r_sum[:, :], ALU.subtract))
            step.link(v.tensor_tensor_scan(grow[:, :], r_a[:, :], r_a[:, :], 0.0, ALU.max, ALU.max))
            v.scalar_tensor_tensor(out=r_f[:, :], in0=r_sum[:, :], scalar=-1.0, in1=grow[:, :],
                                   op0=ALU.mult, op1=ALU.subtract).then_inc(rows_done, 1)
            split(U_QK + 5)

            def logits(n):
                h, i = divmod(n, NB)
                w = (i + 1) * P
                dve.wait_ge(lg_ready, n + 1)
                if i == 0:
                    dve.wait_ge(wb_in[h % 2], 16 * (h // 2 + 1))
                if n >= 3:
                    dve.wait_ge(tr_done, n - 2)
                v.scalar_tensor_tensor(out=lg[n % 3][:, 0:w], in0=ps[n % 2][:, 0:w], scalar=HD ** -0.5,
                                       in1=wb[h % 2][:, S - w:S], op0=ALU.mult, op1=ALU.add).then_inc(lg_done, 1)
                dve.wait_ge(lg_done, n + 1)
                v.tensor_reduce(nmax[:, n:n + 1], lg[n % 3][:, 0:w], AXX, ALU.max, negate=True).then_inc(nmax_done, 1)

            def divide(n):
                h, i = divmod(n, NB)
                p = h // 2
                dve.wait_ge(pv_done, n + 1)
                if n % 8 == 0 and p >= 2:
                    dve.wait_ge(ot_done, p - 1)
                step.link(v.reciprocal(rinv[:, n:n + 1], rsum[:, n:n + 1]))
                v.tensor_scalar(ob[p % 2][:, i, (h % 2) * HD:(h % 2 + 1) * HD], ps[4 + n % 2][:, 0:HD],
                                rinv[:, n:n + 1], None, ALU.mult).then_inc(o_done, 1)

            def conv(t):
                c = t // 2 + MH * (t % 2)
                y, r = cy[t % 2], craw[t % 2]
                dve.wait_ge(pj_ev, G_CONV[t] + 1)
                step.link(v.tensor_scalar(y[:, :], r[:, 0:S], ccol[:, c:c + 1],
                                          ccol[:, CK * KT + c:CK * KT + c + 1], ALU.mult, ALU.add))
                for j in range(1, CK):
                    last = v.scalar_tensor_tensor(out=y[:, :], in0=r[:, j:j + S], scalar=ccol[:, KT * j + c:KT * j + c + 1],
                                                  in1=y[:, :], op0=ALU.mult, op1=ALU.add)
                    if j < CK - 1:
                        step.link(last)
                last.then_inc(conv_y, 1)

            def silu(t):
                y, e = cy[t % 2], craw[t % 2][:, CK - 1:]
                dve.wait_ge(conv_tanh_done, t + 1)
                if t >= 4:
                    dve.wait_ge(kq_done, NB * (t // 2 - 1))
                v.scalar_tensor_tensor(out=qk[t % 4][:, :], in0=e, scalar=1.0, in1=y[:, :],
                                       op0=ALU.add, op1=ALU.mult).then_inc(conv_out, 1)

            for n in range(NA):
                logits(n)
                if n >= 3:
                    divide(n - 3)
                if n == 2:
                    dve.wait_ge(gcol_ready, 1)
                    v.tensor_copy(acol[:, :, :], ps[5][:, 0:16].rearrange("p (b c) -> p b c", b=NB))\
                        .then_inc(acol_done, 1)
                if n % 4 == 2:
                    split(U_QK + 2 + n // 4 + AHEAD)
                if n == 29:
                    conv(0)
            divide(NA - 3)
            silu(0)
            conv(1)
            split(U_VM + 4)
            divide(NA - 2)
            split(U_VM + 5)
            divide(NA - 1)
            silu(1)
            split(U_VM + 6)
            split(U_VM + 7)

            def sigmoid_om(b):
                dve.wait_ge(pj_ev, G_OM + b + 1)
                v.tensor_scalar(om[:, b, :], om[:, b, :], 1.0, 0.5, ALU.add, ALU.mult).then_inc(om_done, 1)

            def weigh(h, j):
                s = NB * h + j
                w = S - j * P
                dve.wait_ge(kq_done, s + 1)
                dve.wait_ge(e_done, s + 1)
                if s < PTS:
                    dve.wait_ge(pv_done, NA + s - PTS + 1)
                else:
                    dve.wait_ge(mpv_done, (s - PTS) // NB + 1)
                v.scalar_tensor_tensor(out=pt[(NA + s) % PTS][:, 0:w], in0=ps[j % 2][:, 0:w], scalar=float(P) ** -0.5 / 4,
                                       in1=ew[j % 2][:, 0:w], op0=ALU.mult, op1=ALU.mult).then_inc(st_done, 1)

            def gated(h):
                dve.wait_ge(mpv_done, h + 1)
                if h == 0:
                    dve.wait_ge(emin_done, 1)
                    dve.wait_ge(om_done, NB)
                if h >= 2:
                    dve.wait_ge(unit_used, U_XK)
                num = [ps[4 + c][:, :].rearrange("p (i c) -> p i c", i=2)[:, :, P] for c in range(2)]
                for c in range(2):
                    step.inc(v.scalar_tensor_tensor(out=den[:, 2 * c:2 * c + 2], in0=num[c], scalar=-1.0,
                                                    in1=emin[:, 2 * c:2 * c + 2, h], op0=ALU.mult, op1=ALU.max))
                dve.wait_ge(v_step, step.k + step.base)
                for c in range(2):
                    step.inc(v.tensor_tensor(den[:, 2 * c:2 * c + 2], num[c], den[:, 2 * c:2 * c + 2], ALU.max))
                dve.wait_ge(v_step, step.k + step.base)
                step.link(v.reciprocal(den[:, :], den[:, :]))
                if h < 2:
                    dve.wait_ge(ot_done, h + 3)
                o = ob[h]
                for i in range(NB):
                    last = v.scalar_tensor_tensor(out=o[:, i, :], in0=ps[4 + i // 2][:, 256 * (i % 2):256 * (i % 2) + P],
                                                  scalar=den[:, i:i + 1], in1=om[:, i, h * P:(h + 1) * P],
                                                  op0=ALU.mult, op1=ALU.mult)
                    if i < NB - 1:
                        step.inc(last)
                last.then_inc(fin1_done, 1)
                dve.wait_ge(v_step, step.k + step.base)
                dve.wait_ge(fin1_done, h + 1)
                for i in range(NB):
                    step.inc(v.bn_stats(hst[:, i, :], o[:, i, :]))
                dve.wait_ge(v_step, step.k + step.base)
                for i in range(NB):
                    last = v.bn_aggr(hmv[:, h, i, :], hst[:, i, :])
                    if i < NB - 1:
                        step.inc(last)
                last.then_inc(hvar_done, 1)

            def head_norm(h):
                o = ob[h]
                dve.wait_ge(v_step, step.k + step.base)
                dve.wait_ge(hr_done, 1 if h < MH - 1 else 2)
                for i in range(NB):
                    step.inc(v.tensor_scalar(o[:, i, :], o[:, i, :], hmv[:, h, i, 0:1], hrs[:, h, i:i + 1],
                                             ALU.subtract, ALU.mult))
                dve.wait_ge(v_step, step.k + step.base)
                gain = mlg[:, h * P:(h + 1) * P].unsqueeze(1).to_broadcast([P, NB, P])
                v.tensor_tensor(o[:, :, :], o[:, :, :], gain, ALU.mult).then_inc(hn_done, 1)

            def mem_lo(b):
                for h in range(2):
                    dve.wait_ge(mhi_done, 2 * b + h + 1)
                    blk = (slice(None), slice(4 * h, 4 * h + 4), slice(b * P, (b + 1) * P))
                    src = ps[6 + h][:, :].rearrange("p (k c) -> p k c", k=4)
                    last = v.tensor_tensor(mtl[blk], src, mth[blk].bitcast(F32), ALU.subtract)
                last.then_inc(mlo_done, 1)

            weigh(0, 0)
            weigh(0, 1)
            split(U_C1 + AHEAD)
            conv(2)
            weigh(0, 2)
            weigh(0, 3)
            split(U_C1 + 1 + AHEAD)
            conv(3)
            silu(2)
            split(U_OM + 4)
            sigmoid_om(0)
            silu(3)
            sigmoid_om(1)
            split(U_OM + 5)
            sigmoid_om(2)
            split(U_OM + 6)
            split(U_OM + 7)
            sigmoid_om(3)
            weigh(1, 0)
            weigh(1, 1)
            gated(0)
            split(U_C2 + AHEAD)
            conv(4)
            weigh(1, 2)
            weigh(1, 3)
            split(U_C2 + 1 + AHEAD)
            conv(5)
            silu(4)
            silu(5)
            split(U_C2 + 2 + AHEAD)
            gated(1)
            conv(6)
            split(U_C2 + 3 + AHEAD)
            silu(6)
            weigh(2, 0)
            weigh(2, 1)
            mem_lo(0)
            weigh(2, 2)
            weigh(2, 3)
            mem_lo(1)
            conv(7)
            silu(7)
            split(U_XK + AHEAD)
            split(U_XK + 1 + AHEAD)
            weigh(3, 0)
            weigh(3, 1)
            gated(2)
            weigh(3, 2)
            weigh(3, 3)
            split(U_XK + 2 + AHEAD)
            for h in range(MH - 1):
                head_norm(h)
                if h < 2:
                    split(U_XK + 3 + h + AHEAD)
            gated(MH - 1)
            split_mt(1, 0)
            split_mt(1, 1)
            for h in range(MH - 1):
                split(U_XK + 5 + h + AHEAD)
                if h < 2:
                    split_mt(1, 2 + h)
            head_norm(MH - 1)
            mt_down(1)

            for k in range(KT):
                split(U_XV + k + AHEAD)
                if k == 4:
                    x_lo(2, 3)
            split(U_XQ + AHEAD)
            split(U_XQ + 1 + AHEAD)
            def row_max(n):
                dve.wait_ge(xl_ready, n + 1)
                v.tensor_reduce(nmax[:, n:n + 1], ps[n % 2][:, 0:MB * P], AXX, ALU.max, negate=True)\
                    .then_inc(xm_done, 1)

            def divide_x(n):
                dve.wait_ge(xe_done, n + 1)
                step.link(v.reciprocal(rinv[:, n:n + 1], rsum[:, n:n + 1]))
                v.tensor_scalar(xp[n % 3][:, :], xp[n % 3][:, :], rinv[:, n:n + 1], None, ALU.mult)\
                    .then_inc(xp_done, 1)

            for n in range(NX + 1):
                if n % NB and n < NX:
                    row_max(n)
                if n >= 1:
                    divide_x(n - 1)
                if n % NB == 0 and n < NX:
                    row_max(n)
                if n % 2 == 1 and n < 12:
                    split(U_XQ + 2 + n // 2 + AHEAD)
                if n in SPLIT_STEPS:
                    split_mt(2, SPLIT_STEPS.index(n))
            mt_down(2)
            x_lo(3, 3)
            ffn_up(1)
            ffn_down(1)


def key_distance_tables(seq, buckets, max_dist, heads):
    import numpy as np
    d = seq - 1 - np.arange(seq + P)
    exact = buckets // 2
    df = np.maximum(d, 1).astype(np.float32)
    large = exact + (np.log(df / np.float32(exact)) / np.float32(math.log(max_dist / exact))
                     * np.float32(buckets - exact)).astype(np.int32)
    bucket = np.where(d < exact, np.maximum(d, 0), np.minimum(large, buckets - 1))
    onehot = (np.arange(buckets)[:, None] == bucket[None, :]).astype(np.float32)
    count = np.zeros(d.shape)
    for window, dilation in ((128, 1), (512, 4), (2048, 16)):
        count += (d >= 0) & (d % dilation == 0) & (d // dilation <= window // dilation)
    row = np.where(count > 0, np.log(np.maximum(count, 1)), -1e30).astype(np.float32)
    return onehot, np.ascontiguousarray(np.broadcast_to(row, (heads, d.size)))


_INS = ['x', 'mem', 'rel_bias', 'ln_g', 'ln_b', 'ffn_w_gate', 'ffn_w_up', 'ffn_w_down', 'w_in', 'conv_w', 'conv_b',
        'ig_bias', 'fg_bias', 'ml_norm_g', 'w_out', 'xq_w', 'xkv_w', 'xo_w']


def kernel(**inputs):
    import numpy as np
    import concourse.bacc as bacc
    from concourse.bass_utils import run_bass_kernel_spmd

    nc = bacc.Bacc("TRN2", target_bir_lowering=False, num_devices=1)
    arrays, args = {}, []
    onehot, lnm = key_distance_tables(inputs['x'].shape[1], inputs['rel_bias'].shape[0], 2048,
                                      inputs['rel_bias'].shape[1])
    named = [(n, np.ascontiguousarray(inputs[n])) for n in _INS] + [('onehot', onehot), ('lnm', lnm)]
    for name, a in named:
        arrays[f"in_{name}"] = a
        args.append(nc.dram_tensor(f"in_{name}", a.shape, mybir.dt.from_np(a.dtype), kind="ExternalInput").ap())
    args.append(nc.dram_tensor("bias_rows", (lnm.shape[0], P, lnm.shape[1]), F32).ap())
    args.append(nc.dram_tensor("g_rows", (inputs['ig_bias'].shape[1], inputs['x'].shape[1]), F32).ap())
    args.append(nc.dram_tensor("out", inputs['x'].shape, F32, kind="ExternalOutput").ap())
    macaron_layer(nc, *args)
    r = run_bass_kernel_spmd(nc, [arrays], core_ids=[0])
    return r.results[0]["out"]
```
